# Optimizing a Trainium2 kernel written in Bass

```python
import math
import jax, jax.numpy as jnp
from jax import lax
import numpy as np

D_MODEL = 1024
BATCH = 1
SEQ = 256
DEPTH = 2

GRID_W = 64
CTX_LEN = 256
DIFF_HEADS = D_MODEL // 256
DIFF_QK_DIM = 64
DIFF_V_DIM = 2 * DIFF_QK_DIM
DIFF_WIDTH = DIFF_HEADS * DIFF_V_DIM
GLA_HEADS = D_MODEL // 256
GLA_DK = 64
GLA_DV = 128
GLA_WIDTH = GLA_HEADS * GLA_DV
GLA_GATE_RANK = 16
GLA_GATE_NORMALIZER = 16.0
GLA_CHUNK = 64
MIX_WIDTH = DIFF_WIDTH + GLA_WIDTH
Q_BLOCK = 128
ROPE_THETA = 10000.0
D_FF = 2816
N_EXPERTS = 8
TOP_K = 2
N_DENSE = (DEPTH + 1) // 2
N_MOE = DEPTH // 2
N_MOD = 6
EPS = 1e-6
IN_SIZES = (2 * DIFF_HEADS * DIFF_QK_DIM, 2 * DIFF_HEADS * DIFF_QK_DIM, DIFF_WIDTH, GLA_HEADS * GLA_DK, GLA_HEADS * GLA_DK, GLA_WIDTH, GLA_WIDTH, 2 * GLA_GATE_RANK)
IN_OFFSETS = tuple(int(o) for o in np.cumsum(IN_SIZES)[:-1])
N_IN = int(sum(IN_SIZES))

kernel_name = 'hybrid_diffattn_gla_moe_dit_block'

def rms_norm(x, g):
    xf = x.astype(jnp.float32)
    y = xf * lax.rsqrt(jnp.mean(xf * xf, axis=-1, keepdims=True) + EPS)
    return (y * g.astype(jnp.float32)).astype(x.dtype)

def rope_tables(n_tokens, dtype):
    rows_n = n_tokens // GRID_W
    row = jnp.repeat(jnp.arange(rows_n), GRID_W).astype(jnp.float32)
    col = jnp.tile(jnp.arange(GRID_W), rows_n).astype(jnp.float32)
    n_freq = DIFF_QK_DIM // 4
    inv = ROPE_THETA ** (-jnp.arange(n_freq, dtype=jnp.float32) / n_freq)
    ang_r = row[:, None] * inv
    ang_c = col[:, None] * inv
    return (jnp.cos(ang_r).astype(dtype), jnp.sin(ang_r).astype(dtype),
            jnp.cos(ang_c).astype(dtype), jnp.sin(ang_c).astype(dtype))

def apply_rot(x, cos, sin):
    x1, x2 = jnp.split(x, 2, axis=-1)
    c = cos[None, :, None, :]
    s = sin[None, :, None, :]
    return jnp.concatenate([x1 * c - x2 * s, x1 * s + x2 * c], axis=-1)

def rope_2d(x, tabs):
    cr, sr, cc, sc = tabs
    half = x.shape[-1] // 2
    return jnp.concatenate([apply_rot(x[..., :half], cr, sr), apply_rot(x[..., half:], cc, sc)], axis=-1)

def diff_attn_core(q1, q2, k1, k2, v, lam):
    scale = DIFF_QK_DIM ** -0.5
    s1 = jnp.einsum('bqhd,bkhd->bhqk', q1, k1).astype(jnp.float32) * scale
    s2 = jnp.einsum('bqhd,bkhd->bhqk', q2, k2).astype(jnp.float32) * scale
    a = jax.nn.softmax(s1, axis=-1) - lam * jax.nn.softmax(s2, axis=-1)
    return jnp.einsum('bhqk,bkhe->bqhe', a.astype(v.dtype), v)

def diff_attn_blocked(q1, q2, k1, k2, v, lam):
    b, s, h, d = q1.shape
    nb = s // Q_BLOCK
    to_blocks = lambda q: q.reshape(b, nb, Q_BLOCK, h, d).transpose(1, 0, 2, 3, 4)
    o = lax.map(lambda qq: diff_attn_core(qq[0], qq[1], k1, k2, v, lam), (to_blocks(q1), to_blocks(q2)))
    return o.transpose(1, 0, 2, 3, 4).reshape(b, s, h, v.shape[-1])

def gla_chunked(q, k, v, glog, s0):
    b, s, h, dk = q.shape
    dv = v.shape[-1]
    C = GLA_CHUNK
    nc = s // C
    f32 = jnp.float32
    qc = q.reshape(b, nc, C, h, dk).astype(f32)
    kc = k.reshape(b, nc, C, h, dk).astype(f32)
    vc = v.reshape(b, nc, C, h, dv).astype(f32)
    g = jnp.cumsum(glog.reshape(b, nc, C, h, dk).astype(f32), axis=2)
    g_last = g[:, :, -1:]
    g_mid = g[:, :, C // 2 - 1:C // 2]
    att = jnp.einsum('bnihk,bnjhk->bnhij', qc * jnp.exp(g - g_mid), kc * jnp.exp(g_mid - g))
    att = jnp.where(jnp.tril(jnp.ones((C, C), dtype=bool)), att, 0.0)
    o_intra = jnp.einsum('bnhij,bnjhv->bnihv', att, vc)
    ds = jnp.einsum('bnjhk,bnjhv->bnhkv', kc * jnp.exp(g_last - g), vc)
    decay = jnp.exp(g_last[:, :, 0])

    def step(state, inp):
        dec, d_s = inp
        return dec[..., None] * state + d_s, state

    s_final, s_prev = lax.scan(step, s0.astype(f32), (jnp.moveaxis(decay, 1, 0), jnp.moveaxis(ds, 1, 0)))
    s_prev = jnp.moveaxis(s_prev, 0, 1)
    o_inter = jnp.einsum('bnihk,bnhkv->bnihv', qc * jnp.exp(g), s_prev)
    o = (o_intra + o_inter).reshape(b, s, h, dv).astype(v.dtype)
    return o, s_final

def gla_bidir(q, k, v, gl_f, gl_b, s0_f, s0_b):
    flip = lambda t: t[:, ::-1]
    o_f, s_f = gla_chunked(q, k, v, gl_f, s0_f)
    o_b, s_b = gla_chunked(flip(q), flip(k), flip(v), flip(gl_b), s0_b)
    return o_f + flip(o_b), s_f, s_b

def gla_gates(glr, gate_w2, gate_b):
    b, s = glr.shape[:2]
    z = jnp.einsum('bsdr,drk->bsdk', glr, gate_w2) + gate_b
    gl = (jax.nn.log_sigmoid(z.astype(jnp.float32)) / GLA_GATE_NORMALIZER).reshape(b, s, 2, GLA_HEADS, GLA_DK)
    return gl[:, :, 0], gl[:, :, 1]

def split_proj(p):
    b, s = p.shape[:2]
    dq, dk, dv, gq, gk, gv, gg, glr = jnp.split(p, IN_OFFSETS, axis=-1)
    dq = dq.reshape(b, s, DIFF_HEADS, 2, DIFF_QK_DIM)
    dk = dk.reshape(b, s, DIFF_HEADS, 2, DIFF_QK_DIM)
    dv = dv.reshape(b, s, DIFF_HEADS, DIFF_V_DIM)
    gq = gq.reshape(b, s, GLA_HEADS, GLA_DK) * (GLA_DK ** -0.5)
    gk = gk.reshape(b, s, GLA_HEADS, GLA_DK)
    gv = gv.reshape(b, s, GLA_HEADS, GLA_DV)
    glr = glr.reshape(b, s, 2, GLA_GATE_RANK)
    return dq[..., 0, :], dq[..., 1, :], dk[..., 0, :], dk[..., 1, :], dv, gq, gk, gv, gg, glr

def token_mixer(h_lat, h_ctx, w_in, gate_w2, gate_b, lam_vec, lam_init, subln_g, onorm_g, w_out, rope_tabs, with_ctx_out):
    f32 = jnp.float32
    lv = lam_vec.astype(f32)
    lam = jnp.exp(jnp.sum(lv[0] * lv[1])) - jnp.exp(jnp.sum(lv[2] * lv[3])) + lam_init
    q1l, q2l, k1l, k2l, vl, gql, gkl, gvl, ggl, glrl = split_proj(h_lat @ w_in)
    q1c, q2c, k1c, k2c, vc, gqc, gkc, gvc, ggc, glrc = split_proj(h_ctx @ w_in)
    q1l, q2l, k1l, k2l = (rope_2d(t, rope_tabs) for t in (q1l, q2l, k1l, k2l))
    k1a = jnp.concatenate([k1c, k1l], axis=1)
    k2a = jnp.concatenate([k2c, k2l], axis=1)
    va = jnp.concatenate([vc, vl], axis=1)
    od_lat = diff_attn_blocked(q1l, q2l, k1a, k2a, va, lam)
    gf_c, gb_c = gla_gates(glrc, gate_w2, gate_b)
    gf_l, gb_l = gla_gates(glrl, gate_w2, gate_b)
    s0 = jnp.zeros((h_ctx.shape[0], GLA_HEADS, GLA_DK, GLA_DV), f32)
    og_ctx, s_f, s_b = gla_bidir(gqc, gkc, gvc, gf_c, gb_c, s0, s0)
    og_lat, _, _ = gla_bidir(gql, gkl, gvl, gf_l, gb_l, s_f, s_b)

    def merge(o_diff, o_gla, g_out):
        b, s = o_diff.shape[:2]
        od = (rms_norm(o_diff, subln_g) * (1.0 - lam_init)).reshape(b, s, DIFF_WIDTH)
        og = rms_norm(o_gla, onorm_g).reshape(b, s, GLA_WIDTH) * jax.nn.silu(g_out)
        return jnp.concatenate([od, og], axis=-1) @ w_out

    y_lat = merge(od_lat, og_lat, ggl)
    y_ctx = None
    if with_ctx_out:
        od_ctx = diff_attn_core(q1c, q2c, k1c, k2c, vc, lam)
        y_ctx = merge(od_ctx, og_ctx, ggc)
    return y_lat, y_ctx

def swiglu(h, w1, w3, w2):
    return (jax.nn.silu(h @ w1) * (h @ w3)) @ w2

def moe_ffn(h, router, w1, w3, w2):
    shape = h.shape
    ht = h.reshape(-1, shape[-1])
    logits = (ht @ router).astype(jnp.float32)
    top_v, top_i = lax.top_k(logits, TOP_K)
    wts = jax.nn.softmax(top_v, axis=-1)
    combine = jnp.sum(jax.nn.one_hot(top_i, N_EXPERTS, dtype=jnp.float32) * wts[..., None], axis=1).astype(h.dtype)

    def expert_step(acc, p):
        e1, e3, e2, cw = p
        return acc + cw[:, None] * swiglu(ht, e1, e3, e2), None

    out, _ = lax.scan(expert_step, jnp.zeros_like(ht), (w1, w3, w2, combine.T))
    return out.reshape(shape)

def setup_inputs(seed: int = 0) -> dict:
    key = jax.random.key(seed)
    ks = jax.random.split(key, 24)
    f32 = jnp.float32
    nrm = lambda k, shape, s: jax.random.normal(k, shape, f32) * s
    gain = lambda k, shape: 1.0 + 0.02 * jax.random.normal(k, shape, f32)
    return {
        'x': nrm(ks[0], (BATCH, SEQ, D_MODEL), 1.0),
        'c': nrm(ks[1], (BATCH, D_MODEL), 1.0),
        'ctx': nrm(ks[2], (BATCH, CTX_LEN, D_MODEL), 1.0),
        'c_ctx': nrm(ks[3], (D_MODEL,), 1.0),
        'w_mod': nrm(ks[4], (DEPTH, D_MODEL, N_MOD * D_MODEL), 0.5 * D_MODEL ** -0.5),
        'b_mod': nrm(ks[5], (DEPTH, N_MOD * D_MODEL), 0.02),
        'g_pre_mix': gain(ks[6], (DEPTH, D_MODEL)),
        'g_post_mix': gain(ks[7], (DEPTH, D_MODEL)),
        'g_pre_ffn': gain(ks[8], (DEPTH, D_MODEL)),
        'g_post_ffn': gain(ks[9], (DEPTH, D_MODEL)),
        'w_in': nrm(ks[10], (DEPTH, D_MODEL, N_IN), D_MODEL ** -0.5),
        'gla_gate_w2': nrm(ks[11], (DEPTH, 2, GLA_GATE_RANK, GLA_HEADS * GLA_DK), GLA_GATE_RANK ** -0.5),
        'gla_gate_b': nrm(ks[12], (DEPTH, 2, GLA_HEADS * GLA_DK), 0.1),
        'diff_lambda': nrm(ks[13], (DEPTH, 4, DIFF_QK_DIM), 0.1),
        'diff_subln': gain(ks[14], (DEPTH, DIFF_V_DIM)),
        'gla_onorm': gain(ks[15], (DEPTH, GLA_DV)),
        'w_out': nrm(ks[16], (DEPTH, MIX_WIDTH, D_MODEL), MIX_WIDTH ** -0.5),
        'ffn_w1': nrm(ks[17], (N_DENSE, D_MODEL, D_FF), D_MODEL ** -0.5),
        'ffn_w3': nrm(ks[18], (N_DENSE, D_MODEL, D_FF), D_MODEL ** -0.5),
        'ffn_w2': nrm(ks[19], (N_DENSE, D_FF, D_MODEL), D_FF ** -0.5),
        'router': nrm(ks[20], (N_MOE, D_MODEL, N_EXPERTS), D_MODEL ** -0.5),
        'moe_w1': nrm(ks[21], (N_MOE, N_EXPERTS, D_MODEL, D_FF), D_MODEL ** -0.5),
        'moe_w3': nrm(ks[22], (N_MOE, N_EXPERTS, D_MODEL, D_FF), D_MODEL ** -0.5),
        'moe_w2': nrm(ks[23], (N_MOE, N_EXPERTS, D_FF, D_MODEL), D_FF ** -0.5),
    }

def reference(x, c, ctx, c_ctx, w_mod, b_mod, g_pre_mix, g_post_mix, g_pre_ffn, g_post_ffn, w_in, gla_gate_w2, gla_gate_b, diff_lambda, diff_subln, gla_onorm, w_out, ffn_w1, ffn_w3, ffn_w2, router, moe_w1, moe_w3, moe_w2):
    rope_tabs = rope_tables(x.shape[1], x.dtype)
    silu_c = jax.nn.silu(c)
    silu_cc = jax.nn.silu(c_ctx)
    xc = ctx
    for l in range(DEPTH):
        last = l == DEPTH - 1
        lam_init = 0.8 - 0.6 * math.exp(-0.3 * l)
        sh1, sc1, gt1, sh2, sc2, gt2 = (m[:, None] for m in jnp.split(silu_c @ w_mod[l] + b_mod[l], N_MOD, axis=-1))
        csh1, csc1, cgt1, csh2, csc2, cgt2 = jnp.split(silu_cc @ w_mod[l] + b_mod[l], N_MOD, axis=-1)
        h = rms_norm(x, g_pre_mix[l]) * (1.0 + sc1) + sh1
        hc = rms_norm(xc, g_pre_mix[l]) * (1.0 + csc1) + csh1
        y, yc = token_mixer(h, hc, w_in[l], gla_gate_w2[l], gla_gate_b[l], diff_lambda[l], lam_init,
                            diff_subln[l], gla_onorm[l], w_out[l], rope_tabs, not last)
        x = x + gt1 * rms_norm(y, g_post_mix[l])
        if not last:
            xc = xc + cgt1 * rms_norm(yc, g_post_mix[l])
        if l % 2 == 0:
            ffn = lambda t, i=l // 2: swiglu(t, ffn_w1[i], ffn_w3[i], ffn_w2[i])
        else:
            ffn = lambda t, i=l // 2: moe_ffn(t, router[i], moe_w1[i], moe_w3[i], moe_w2[i])
        h = rms_norm(x, g_pre_ffn[l]) * (1.0 + sc2) + sh2
        x = x + gt2 * rms_norm(ffn(h), g_post_ffn[l])
        if not last:
            hc = rms_norm(xc, g_pre_ffn[l]) * (1.0 + csc2) + csh2
            xc = xc + cgt2 * rms_norm(ffn(hc), g_post_ffn[l])
    return x


_drawn_inputs = setup_inputs


def setup_inputs(seed=0):
    import zlib

    import numpy as np

    out = dict(_drawn_inputs(seed))
    spreads = {}
    factors = {'g_pre_mix': 3.208,
     'g_post_mix': 4.336,
     'g_post_ffn': 5.976,
     'diff_lambda': 2.978,
     'diff_subln': 4.358,
     'gla_onorm': 3.93}
    for name, (base, spread) in spreads.items():
        noise = np.random.default_rng([zlib.crc32(name.encode()), seed]).standard_normal(out[name].shape)
        drawn = base * np.exp(spread * noise) if base else spread * noise
        out[name] = __import__('jax').numpy.asarray(drawn.astype(out[name].dtype))
    for name, factor in factors.items():
        out[name] = (out[name] * factor).astype(out[name].dtype)
    return out
```

```python
from contextlib import ExitStack

import concourse.bass as bass
from concourse import mybir

F32 = mybir.dt.float32
F32R = mybir.dt.float32r
I32 = mybir.dt.int32
ACT = mybir.ActivationFunctionType
ALU = mybir.AluOpType
X_AXIS = mybir.AxisListType.X

P = 128
D_MODEL, CTX, LAT, DEPTH = 1024, 256, 256, 2
T = CTX + LAT
TILES = T // P
KT = D_MODEL // P
HEADS, QK, VD = 4, 64, 128
WIDTH = HEADS * VD
RANK = 16
CHUNK = 64
D_FF = 2816
FT = D_FF // P
EXPERTS = 8
N_MOD = 6
GRID_W = 64
ROPE_THETA = 10000.0
EPS = 1e-6
LAM_INIT = (0.2, 0.35550906759096937)

UNIT = 2048
RING = 3
MOD_A = 2 * D_MODEL // 256
MOD_UNITS = N_MOD * D_MODEL // 256
IN_F, IN_K = 6, 6
OUT_UNITS = D_MODEL // 256
UP_UNITS, DOWN_UNITS = FT, FT // 2
FC = D_FF // 256
EXPERT_UNITS = 3 * FC


def unit_numbers():
    at, n = {}, 0
    for l in range(DEPTH):
        for stage, count in (("mod_a", MOD_A), ("in", IN_F + IN_K), ("mod_b", MOD_UNITS - MOD_A),
                             ("out", OUT_UNITS)):
            at[stage, l] = n
            n += count
        if l == 0:
            at["up", l] = n
            n += UP_UNITS
            at["down", l] = n
            n += DOWN_UNITS
        else:
            at["moe", l] = n
            n += EXPERTS * EXPERT_UNITS
    return at, n


U, N_UNITS = unit_numbers()

C_IDENT, C_TRI, C_UPPER, C_ONES, C_PERM, C_IOTA = 0, 128, 384, 512, 640, 768
C_SELB, C_SELC, C_EPS, C_DESC, N_CONST = 1024, 1280, 1282, 1283, 1296
V_C, V_CC = 0, 8
V_LAYER, V_STRIDE = 16, 66
V_GPM, V_GPF, V_SUB, V_ON, V_BMOD = 0, 8, 16, 17, 18
N_COLS = V_LAYER + DEPTH * V_STRIDE + 4


def token_tiles(l, stage):
    return range(TILES) if l == 0 or stage == "mix" else range(CTX // P, TILES)


def mod_steps(part):
    units = range(MOD_A) if part == "a" else range(MOD_A, MOD_UNITS)
    for j in units:
        yield "mod", j
        if j > units[0]:
            yield "modx", j - 1
    yield "modx", units[-1]


def is_gate(j):
    return (j // 4) in (2, 5)


def chunk_order(d):
    n = CTX // CHUNK
    return list(range(2 * n)) if d == 0 else list(range(n))[::-1] + list(range(n, 2 * n))[::-1]


def expert_steps():
    steps, m = [], 0
    for c in range(FC + 2):
        here = {}
        if c < FC:
            here["up"] = (m, m + 1)
            m += 2
        if c >= 2:
            here["down"] = m
            m += 1
        steps.append(here)
    assert m == EXPERT_UNITS
    return steps


STEPS = expert_steps()


def attn_items(l):
    return [(h, t) for t in token_tiles(l, "out") for h in range(HEADS)]


def gla_items(l):
    return [(h, t) for t in token_tiles(l, "out") for h in range(HEADS)]


def psum_jobs():
    out = []
    for l in range(DEPTH):
        out += [(kind, l, j) for kind, j in mod_steps("a")]
        out += [("T", l, "mix", k) for k in range(KT)]
        out += [("F", l, f) for f in range(2 * IN_F)]
        out += [("K", l, u, g) for u in range(IN_K) for g in range(2)]
        out += [("glr", l), ("glrT", l)]
        out += [("rope", l, b) for b in range(4)]
        n = len(attn_items(l))
        for i in range(n + 2):
            if i < n:
                out += [("S", l, i, 0), ("S", l, i, 1)]
            if 1 <= i <= n:
                out.append(("PT", l, i - 1))
            if i >= 2:
                out.append(("O", l, i - 2))
        out += [("Z", l, t) for t in range(TILES)]
        out += [("G", l, dp) for dp in range(4)]
        for dp in range(4):
            out += [("KT", l, dp), ("DS", l, dp, 0), ("DS", l, dp, 1)]
        m = len(gla_items(l))
        for i in range(m + 1):
            if i < m:
                out.append(("M", l, i))
            if i >= 1:
                out.append(("OG", l, i - 1))
        out += [(kind, l, j) for kind, j in mod_steps("b")]
        out += [("MT", l, f) for f in range(KT)]
        out += [("Y", l, u, g) for u in range(OUT_UNITS) for g in range(2 if l == 0 else 1)]
        out += [("T", l, "ffn", k) for k in range(KT)]
        if l == 0:
            for j in range(UP_UNITS):
                out += [("GU", l, j, 0), ("GU", l, j, 1)]
            out += [("D", l, t, h) for t in range(TILES) for h in range(2)]
        else:
            out += [("H2", q) for q in range(4)] + [("LG",), ("POS",)]
    return {key: n for n, key in enumerate(out)}


JOBS = psum_jobs()
BANKS = 8

BASE = 16512
A_RAW, A_HI, A_LO = 0, 6144, 12288
A_X = 18432
A_ACTT = 22528
A_GATE = 30720
A_V, A_GV, A_GG, A_GQ, A_GK = 34816, 36864, 38912, 40960, 41984
A_GL, A_GT, A_OD, A_GLRT = 43008, 45056, 47104, 49152
A_CONST = 49664
A_COLS = A_CONST + N_CONST
A_WSM = A_COLS + N_COLS
A_GW2 = A_WSM + 576
A_AM = A_GW2 + 512
A_STAT = A_AM + 512
A_ROUTE = A_OD + 1024
A_AT, A_ATS, A_SIL = A_V, 46080, 48128


def release_points():
    at = {}
    for l in range(DEPTH):
        for j in range(MOD_UNITS):
            at[(U["mod_a", l] + j) if j < MOD_A else (U["mod_b", l] + j - MOD_A)] = ("job", JOBS["mod", l, j])
        for u in range(IN_F):
            at[U["in", l] + u] = ("job", JOBS["F", l, 2 * u + 1])
        for u in range(IN_K):
            at[U["in", l] + IN_F + u] = ("job", JOBS["K", l, u, 1])
        for u in range(OUT_UNITS):
            at[U["out", l] + u] = ("job", JOBS["Y", l, u, 1 if l == 0 else 0])
    for j in range(UP_UNITS):
        at[U["up", 0] + j] = ("job", JOBS["GU", 0, j, 1])
    for i in range(DOWN_UNITS):
        at[U["down", 0] + i] = ("tile", 2 * i + 1) if i < DOWN_UNITS - 1 else ("job", JOBS["D", 0, TILES - 1, 1])
    return at


RELEASE = release_points()
PASSES = ((0, 0), (0, 1), (1, 0))


def n_keys(t):
    return CTX if t < CTX // P else T


TURN_BANK = 3


def up_bank(c, tau):
    return c % 2 if tau == 0 else 2


def build(nc, ctx, units, x_in, ctx_in, const_in, cols_in, wsm_in, gw2_in, lam_in, rope_in, aux_in, out):
    def at(name, offset, shape, dt=F32):
        size = 1
        for s in shape[1:]:
            size *= s
        return nc.alloc_sbuf_tensor_at(name, shape, dt, offset=BASE + 4 * offset)

    stat_at = [A_STAT]

    def stat(name, n, dt=F32):
        here = stat_at[0]
        stat_at[0] += -(-n // 8) * 8
        return at(name, here, [P, n], dt)

    raw = at("raw", A_RAW, [P, RING, UNIT])
    w_hi = at("w_hi", A_HI, [P, RING, UNIT], F32R)
    w_lo = at("w_lo", A_LO, [P, RING, UNIT], F32R)
    X = at("X", A_X, [P, TILES, D_MODEL])
    act_hi = at("act_hi", A_ACTT, [P, KT, T], F32R)
    act_lo = at("act_lo", A_ACTT + 4096, [P, KT, T], F32R)
    gexp = at("gexp", A_ACTT, [P, 4, 4, T])
    y_ffn = at("y_ffn", A_ACTT, [P, TILES, D_MODEL])
    gate = at("gate", A_GATE, [P, 2, 2, D_MODEL])
    qT = at("qT", A_GATE, [P, HEADS, T])
    kT = at("kT", A_GATE + 2048, [P, HEADS, T])
    states = at("states", A_GATE, [P, 4, 8, VD])
    v = at("v", A_V, [P, TILES, WIDTH])
    og = at("og", A_V, [P, TILES, WIDTH])
    gv = at("gv", A_GV, [P, TILES, WIDTH])
    gg = at("gg", A_GG, [P, TILES, WIDTH])
    y_mix = at("y_mix", A_GV, [P, TILES, D_MODEL])
    aux = at("aux", A_GV, [4, 2, 2 * D_MODEL])
    xn = at("xn", A_V, [P, TILES, D_MODEL])
    gqT = at("gqT", A_GQ, [P, 2, T])
    gkT = at("gkT", A_GK, [P, 2, T])
    gl = at("gl", A_GL, [P, TILES, T])
    zabs = at("zabs", A_GT, [P, TILES, T])
    GT = at("GT", A_GT, [P, 4, T])
    klT = at("klT", A_GL, [P, 4, TILES, P])
    gla_junk = at("gla_junk", A_GT, [P, P])
    probs = at("probs", A_GL, [P, 2, 2, T])
    probsT = at("probsT", A_GL + 2048, [P, 2, T])
    att_junk = at("att_junk", A_GL + 3072, [P, P])
    rope = at("rope", A_GL + 3584, [P, 2, LAT])
    hf = at("hf", A_GL, [P, RING, T])
    y_junk = at("y_junk", A_GL, [P, D_MODEL])
    glr_hi = at("glr_hi", A_GL + 1536, [P, KT, 32], F32R)
    glr_lo = at("glr_lo", A_GL + 1792, [P, KT, 32], F32R)
    glr_tok = at("glr_tok", A_GL + 2048, [P, TILES, 32])
    rope_tmp = at("rope_tmp", A_GL + 2176, [P, 2, LAT])
    c_cols = at("c_cols", A_GL + 3072, [P, KT, P], F32R)
    lam_in_sb = at("lam_in_sb", A_GL, [P, DEPTH, 2, 2, QK])
    lam_prod = at("lam_prod", A_GL + 512, [P, DEPTH, 2, QK])
    mod_row = at("mod_row", A_OD, [4, 2, 256])
    mod_row_b = at("mod_row_b", A_GQ, [4, 2, 256])
    od = at("od", A_OD, [P, TILES, WIDTH])
    glrT = at("glrT", A_GLRT, [33, T])
    const = at("const", A_CONST, [P, N_CONST])
    cols = at("cols", A_COLS, [P, N_COLS])
    wsm = at("wsm", A_WSM, [P, 576])
    gw2 = at("gw2", A_GW2, [33, T])
    Am = at("Am", A_AM, [P, 2, 2, P])
    ffnT = at("ffnT", A_AT, [P, FT, T])
    ffn_hi = at("ffn_hi", A_ATS, [P, 2, T], F32R)
    ffn_lo = at("ffn_lo", A_ATS + 1024, [P, 2, T], F32R)
    ffn_sil = at("ffn_sil", A_SIL, [P, 2, T])

    xt_hi = at("xt_hi", A_ACTT, [P, KT, 2, P], F32R)
    xt_lo = at("xt_lo", A_ACTT + 2048, [P, KT, 2, P], F32R)
    h2_hi = at("h2_hi", A_ACTT + 4096, [P, 2, D_MODEL], F32R)
    h2_lo = at("h2_lo", A_ACTT + 6144, [P, 2, D_MODEL], F32R)
    h2T = at("h2T", A_GG, [P, KT, LAT])
    y_moe = at("y_moe", A_GQ, [P, 2, D_MODEL])
    e_sil = at("e_sil", A_GL, [P, 2, 256])
    e_act = at("e_act", A_V, [P, 2, 2, 256])
    sel = at("sel", A_GL + 1024, [P, 2, 2 * P], F32R)
    selT = at("selT", A_GL + 1536, [P, 2, P], F32R)
    eT_hi = at("eT_hi", A_GL + 1792, [P, 2, 2, 256], F32R)
    eT_lo = at("eT_lo", A_GL + 2816, [P, 2, 2, 256], F32R)
    route = at("route", A_GL + 3840, [P, 2, 6, EXPERTS])
    ey_hi = at("ey_hi", A_OD, [P, D_MODEL], F32R)
    ey_lo = at("ey_lo", A_OD + 1024, [P, D_MODEL], F32R)

    c_act = stat("c_act", 16)
    ssq, std, rstd = stat("ssq", 4), stat("std", 4), stat("rstd", 4)
    modc = at("modc", stat_at[0], [P, 2, 2, KT, 2])
    stat_at[0] += 64
    od_ssq, od_std, od_rstd = stat("od_ssq", 16), stat("od_std", 16), stat("od_rstd", 16)
    og_ssq, og_std, og_rstd = stat("og_ssq", 16), stat("og_std", 16), stat("og_rstd", 16)
    sub_gain = stat("sub_gain", DEPTH)
    row_max, neg_max, row_sum, row_inv = (at(n, stat_at[0] + 8 * i, [P, 2, 2]) for i, n in
                                          enumerate(("row_max", "neg_max", "row_sum", "row_inv")))
    stat_at[0] += 32
    neg_lam, lam_sum, lam_exp = stat("neg_lam", 2), stat("lam_sum", 4), stat("lam_exp", 4)
    decay = at("decay", stat_at[0], [P, 4, 8])
    stat_at[0] += 32
    e_cols = stat("e_cols", 6)
    counts_i = stat("counts_i", EXPERTS, I32)

    psum = nc.alloc_psum_tensor("psum", [P, BANKS, 512], F32)

    ident, ones = const[:, C_IDENT:C_IDENT + P], const[:, C_ONES:C_ONES + P]
    tri = const[:, C_TRI:C_TRI + 2 * P]
    eps = const[:, C_EPS:C_EPS + 1]

    sems = {}

    def sem(name):
        if name not in sems:
            sems[name] = nc.alloc_semaphore(name)
        return sems[name]

    loaded, x_loaded, rope_loaded, gw2_loaded, aux_loaded, stored = (
        sem(n) for n in ("loaded", "x_loaded", "rope_loaded", "gw2_loaded", "aux_loaded", "stored"))
    arrived = [sem(f"arrived{s}") for s in range(RING)]
    hi_ready, lo_ready, units_used = sem("hi_ready"), sem("lo_ready"), sem("units_used")
    filled = sem("filled")
    emptied = [sem(f"emptied{b}") for b in range(BANKS)]

    def bank(key):
        return psum[:, JOBS[key] % BANKS, :]

    def wait_filled(eng, key):
        eng.wait_ge(filled, JOBS[key] + 1)

    def wait_copied(eng, key):
        eng.wait_ge(emptied[JOBS[key] % BANKS], JOBS[key] // BANKS + 1)

    def wait_emptied(pe, key):
        if JOBS[key] >= BANKS:
            pe.wait_ge(emptied[JOBS[key] % BANKS], JOBS[key] // BANKS)

    def wait_released(eng, n):
        kind, count = RELEASE[n]
        eng.wait_ge(filled if kind == "job" else sem("down_tiles"), count + 1)

    def esem(name, tau):
        return sem(f"e_{name}{tau}")

    def wait_expert_unit_used(eng, e, m):
        before = m < 0
        m %= EXPERT_UNITS
        for c, here in enumerate(STEPS):
            for name, unit, chunk in (("half", here.get("up", (-1,))[0], c), ("up", here.get("up", (-1,))[-1], c),
                                      ("down", here.get("down", -1), c - 2)):
                if unit == m:
                    for tau in range(2):
                        eng.wait_ge(esem(name, tau), (e + (0 if before else 1)) * FC + (chunk + 1))

    def both(eng, many, work, signals):
        work(0)
        with eng.If(many):
            work(1)
            eng.nop()
        with eng.Else():
            for name, count in signals:
                eng.sem_inc(esem(name, 1), count)

    rt = stat("rt", 12)
    assert BASE + 4 * stat_at[0] <= nc.sbuf_usable_end, stat_at[0]
    weights, acts = (w_hi, w_lo), (act_hi, act_lo)
    y_mix_of, y_ffn_of, y_moe_of = (lambda t: y_mix[:, t, :]), (lambda t: y_ffn[:, t, :]), (lambda t: y_moe[:, t - 2, :])

    block = ctx.enter_context(nc.Block())

    @block.sync
    def _(sp):
        def load(slot, n):
            sp.dma_start(raw[:, slot, :], units[bass.ds(n, 1)].rearrange("a p n -> (a p) n")).then_inc(arrived[slot], 16)

        for n in range(RING):
            load(n, n)
        rounds = N_UNITS // RING
        with sp.Fori(1, rounds) as i:
            for s in range(RING):
                sp.wait_ge(lo_ready, i * RING + (s - RING + 1))
                load(s, i * RING + s)
        for n in range(rounds * RING, N_UNITS):
            sp.wait_ge(lo_ready, n - RING + 1)
            load(n % RING, n)
        sp.wait_ge(sem("x_ffn1"), 2)
        sp.dma_start(out[0].rearrange("(t p) d -> p t d", p=P), X[:, CTX // P:TILES, :]).then_inc(stored, 16)
        sp.wait_ge(stored, 16)

    @block.gpsimd
    def _(pool):
        pool.memset(Am[:, :, :, :], 0.0).then_inc(sem("zeros"), 1)
        pool.wait_ge(sem("zeros"), 1)
        pool.memset(glrT[32:33, :], 1.0).then_inc(sem("zeros"), 1)
        pool.wait_ge(sem("zeros"), 2)
        for l in range(DEPTH):
            pool.wait_ge(sem("lam_ready") if l == 0 else sem("x_ffn0"), 1 if l == 0 else TILES)
            pool.memset(c_cols[:, :, :].bitcast(F32), 0.0).then_inc(sem("c_zero"), 1)
            pool.wait_ge(filled, JOBS["T", l, "mix", 0] + 1)
            pool.dma_start(rope[:, :, :], rope_in).then_inc(rope_loaded, 16)
            if l == 1:
                pool.wait_ge(filled, JOBS["Z", 0, TILES - 1] + 1)
            pool.dma_start(gw2[:, :], gw2_in[l]).then_inc(gw2_loaded, 16)
            pool.wait_ge(sem(f"gexp{l}"), 16)
            pool.memset(c_cols[:, :, :].bitcast(F32), 0.0).then_inc(sem("c_zero"), 1)
            pool.wait_ge(sem(f"merged{l}"), 2)
            pool.dma_start(aux[:, :, :], aux_in[l]).then_inc(aux_loaded, 16)

    @block.scalar
    def _(act):
        split = [0]

        def split_upto(n):
            while split[0] <= min(n, U["moe", 1] - 1):
                i = split[0]
                act.wait_ge(arrived[i % RING], 16 * (i // RING + 1))
                if i >= RING:
                    wait_released(act, i - RING)
                act.activation(w_hi[:, i % RING, :], raw[:, i % RING, :], ACT.Copy).then_inc(hi_ready, 1)
                split[0] += 1

        def copy_out(key, dst, src, scale=1.0):
            wait_filled(act, key)
            act.activation(dst, src, ACT.Copy, scale=scale).then_inc(emptied[JOBS[key] % BANKS], 1)

        for dst, src in ((const, const_in), (cols, cols_in), (wsm, wsm_in)):
            act.dma_start(dst[:, :], src).then_inc(loaded, 16)
        act.dma_start(lam_in_sb[:, :, :, :, :].rearrange("p a b c d -> p (a b c d)"),
                      lam_in.to_broadcast([P, DEPTH * 4 * QK])).then_inc(loaded, 16)
        for i, src in enumerate((ctx_in, x_in)):
            act.dma_start(X[:, 2 * i:2 * i + 2, :],
                          src.rearrange("(t p) d -> p t d", p=P)).then_inc(x_loaded, 16)
        act.wait_ge(loaded, 64)
        act.activation(c_act[:, :], cols[:, 0:16], ACT.Silu).then_inc(sem("c_act"), 1)
        act.wait_ge(sem("lam_sum"), 1)
        act.activation(lam_exp[:, :], lam_sum[:, :], ACT.Exp).then_inc(sem("lam_exp"), 1)

        def modulation(l, part):
            u0 = U[f"mod_{part}", l] - (0 if part == "a" else MOD_A)
            n = 2 * l + (part == "b")
            act.wait_ge(sem("c_act"), 1)
            act.wait_ge(sem("c_zero"), n + 1)
            for i in range(2):
                act.activation(c_cols[:, :, 2 * i], c_act[:, 8 * i:8 * i + 8], ACT.Copy).then_inc(sem("c_hi"), 1)
            row = mod_row if part == "a" else mod_row_b
            for kind, j in mod_steps(part):
                if kind == "mod":
                    split_upto(u0 + j + 2)
                    if not is_gate(j):
                        if j - 2 >= (0 if part == "a" else MOD_A):
                            wait_filled(act, ("modx", l, j - 2))
                        copy_out(("mod", l, j), row[:, j % 2, :], bank(("mod", l, j))[0:4, 0:256])
                elif is_gate(j):
                    key = ("modx", l, j)
                    copy_out(key, gate[:, 0 if j < 12 else 1, :, (j % 4) * 256:(j % 4 + 1) * 256],
                             bank(key).rearrange("p (s n) -> p s n", s=2))

        def mean_square(name, l, stage, tiles, src, junk, wait):
            done = sem(f"{name}_{stage}{l}")
            for n, t in enumerate(tiles):
                wait(n)
                if n:
                    act.wait_ge(done, n)
                act.activation(junk(t), src(t), ACT.Square, accum_out=ssq[:, t:t + 1]).then_inc(done, 1)
            act.wait_ge(done, len(tiles))
            act.activation(std[:, tiles[0]:TILES], ssq[:, tiles[0]:TILES], ACT.Sqrt, bias=eps,
                           scale=1.0 / D_MODEL).then_inc(done, 1)

        def norm(l, stage):
            tiles = token_tiles(l, stage)
            source, count = {("mix", 0): (x_loaded, 32), ("mix", 1): (sem("x_ffn0"), TILES),
                             ("ffn", 0): (sem("x_mix0"), TILES), ("ffn", 1): (sem("x_mix1"), 2)}[stage, l]
            mean_square("norm", l, stage, tiles, lambda t: X[:, t, :], lambda t: xn[:, t, :],
                        lambda n: act.wait_ge(source, count))

        def halves(l, stage):
            return (0, 1) if l == 0 or stage == "mix" else (1,)

        def modulated(l, stage):
            w = 0 if stage == "mix" else 1
            act.wait_ge(sem(f"scale{l}"), 4 * (w + 1))
            for k in range(KT):
                key = ("T", l, stage, k)
                wait_filled(act, key)
                sides = halves(l, stage)
                if k >= RING and len(sides) == 2:
                    act.wait_ge(sem(f"act_lo_{stage}{l}"), k - RING + 1)
                for s in sides:
                    dst = h2T[:, k, :] if len(sides) == 1 else hf[:, k % RING, s * 256:(s + 1) * 256]
                    ins = act.activation(dst, bank(key)[:, s * 256:(s + 1) * 256], ACT.Identity,
                                         scale=modc[:, w, 1, k, s:s + 1], bias=modc[:, w, 0, k, s:s + 1])
                ins.then_inc(emptied[JOBS[key] % BANKS], 1)
                if len(sides) == 2:
                    wait_copied(act, key)
                    act.activation(act_hi[:, k, :], hf[:, k % RING, :], ACT.Copy).then_inc(sem(f"act_hi_{stage}{l}"), 1)

        def in_projection(l):
            act.activation(glr_hi[:, :, :], wsm[:, l * 256:(l + 1) * 256].rearrange("p (k n) -> p k n", n=32),
                           ACT.Copy).then_inc(sem(f"glr_hi{l}"), 1)
            for u in range(IN_F):
                split_upto(U["in", l] + u + 2)
                for f in (2 * u, 2 * u + 1):
                    dst = (qT[:, f, :] if f < 4 else kT[:, f - 4, :] if f < 8 else
                           gqT[:, f - 8, :] if f < 10 else gkT[:, f - 10, :])
                    copy_out(("F", l, f), dst, bank(("F", l, f)), QK ** -0.5 if f in (8, 9) else 1.0)
            for u in range(IN_K):
                split_upto(U["in", l] + IN_F + u + 2)
                for g in range(2):
                    dst = (v, gv, gg)[u // 2][:, 2 * g:2 * g + 2, (u % 2) * 256:(u % 2 + 1) * 256]
                    key = ("K", l, u, g)
                    copy_out(key, dst, bank(key).rearrange("p (t n) -> p t n", t=2))
            copy_out(("glr", l), glr_tok[:, :, :].rearrange("p t n -> p (t n)"), bank(("glr", l))[:, 0:P])

        def attention(l):
            items = attn_items(l)
            n = len(items)
            for i in range(n + 2):
                if i < n:
                    b, keys = i % 2, n_keys(items[i][1])
                    act.wait_ge(sem(f"neg_max{l}"), i + 1)
                    if i >= 2:
                        wait_filled(act, ("PT", l, i - 2))
                    for j in range(2):
                        act.activation(probs[:, b, j, 0:keys], bank(("S", l, i, j))[:, 0:keys], ACT.Exp,
                                       scale=QK ** -0.5, bias=neg_max[:, b, j:j + 1],
                                       accum_out=row_sum[:, b, j:j + 1]).then_inc(
                                           emptied[JOBS["S", l, i, j] % BANKS], 1)
                if 1 <= i <= n:
                    key, keys = ("PT", l, i - 1), n_keys(items[i - 1][1])
                    if i >= 3:
                        wait_filled(act, ("O", l, i - 3))
                    copy_out(key, probsT[:, (i - 1) % 2, 0:keys], bank(key)[:, 0:keys])
                if i >= 2:
                    key, (h, t) = ("O", l, i - 2), items[i - 2]
                    wait_filled(act, key)
                    act.activation(od[:, t, h * P:(h + 1) * P], bank(key)[:, 0:P], ACT.Copy)
                    if i >= 3:
                        wait_copied(act, ("O", l, i - 3))
                    act.activation(att_junk[:, :], bank(key)[:, 0:P], ACT.Square,
                                   accum_out=od_ssq[:, 4 * t + h:4 * t + h + 1]).then_inc(
                                       emptied[JOBS[key] % BANKS], 1)

        def head_std(l, dst, src, last):
            t0 = 4 * token_tiles(l, "out")[0]
            wait_copied(act, last)
            act.activation(dst[:, t0:16], src[:, t0:16], ACT.Sqrt, bias=eps, scale=1.0 / VD).then_inc(sem(f"head_std{l}"), 1)

        def gla(l):
            done = sem(f"gate_log{l}")
            for t in range(TILES):
                wait_filled(act, ("Z", l, t))
                if t == 0:
                    act.wait_ge(sem(f"merged{l}"), 1)
                act.activation(zabs[:, t, :], bank(("Z", l, t)), ACT.Abs).then_inc(sem(f"zabs{l}"), 1)
            for t in range(TILES):
                act.wait_ge(sem(f"zabs{l}"), t + 1)
                act.activation(zabs[:, t, :], zabs[:, t, :], ACT.Exp, scale=-1.0).then_inc(done, 1)
            act.wait_ge(done, TILES)
            for t in range(TILES):
                act.activation(zabs[:, t, :], zabs[:, t, :], ACT.Ln, bias=const[:, C_ONES:C_ONES + 1]).then_inc(done, 1)
            for dp in range(4):
                copy_out(("G", l, dp), GT[:, dp, :], bank(("G", l, dp)))
            done = sem(f"gexp{l}")
            for dp in range(4):
                act.wait_ge(sem(f"gsub{l}"), 2 * dp + 2)
                act.activation(gexp[:, 1, dp, :], gexp[:, 0, dp, :], ACT.Exp, scale=-1.0).then_inc(done, 1)
                act.activation(gexp[:, 2, dp, :], gexp[:, 2, dp, :], ACT.Exp).then_inc(done, 1)
                act.activation(gexp[:, 3, dp, :], GT[:, dp, :], ACT.Exp).then_inc(done, 1)
                act.wait_ge(done, 4 * dp + 1)
                act.activation(gexp[:, 0, dp, :], gexp[:, 0, dp, :], ACT.Exp).then_inc(done, 1)
            for dp in range(4):
                copy_out(("KT", l, dp), klT[:, dp, :, :].rearrange("p t n -> p (t n)"), bank(("KT", l, dp)))
            t0 = token_tiles(l, "out")[0]
            act.activation(gg[:, t0:TILES, :], gg[:, t0:TILES, :], ACT.Silu).then_inc(sem(f"gg_silu{l}"), 1)
            for i, (h, t) in enumerate(gla_items(l)):
                key = ("OG", l, i)
                wait_filled(act, key)
                act.activation(og[:, t, h * P:(h + 1) * P], bank(key)[:, 0:P], ACT.Copy)
                if i >= 1:
                    wait_copied(act, ("OG", l, i - 1))
                act.activation(gla_junk[:, :], bank(key)[:, 0:P], ACT.Square,
                               accum_out=og_ssq[:, 4 * t + h:4 * t + h + 1]).then_inc(emptied[JOBS[key] % BANKS], 1)
            head_std(l, og_std, og_ssq, ("OG", l, len(gla_items(l)) - 1))

        def merged(l):
            lo = token_tiles(l, "out")[0] * P
            for f in range(KT):
                key = ("MT", l, f)
                wait_filled(act, key)
                if f >= RING:
                    act.wait_ge(sem(f"act_lo_out{l}"), f - RING + 1)
                gain = sub_gain[:, l:l + 1] if f < 4 else cols[:, V_LAYER + l * V_STRIDE + V_ON:][:, 0:1]
                act.activation(hf[:, f % RING, lo:T], bank(key)[:, lo:T], ACT.Copy, scale=gain).then_inc(
                    emptied[JOBS[key] % BANKS], 1)
                wait_copied(act, key)
                act.activation(act_hi[:, f, lo:T], hf[:, f % RING, lo:T], ACT.Copy).then_inc(sem(f"act_hi_out{l}"), 1)

        def out_projection(l):
            for u in range(OUT_UNITS):
                split_upto(U["out", l] + u + 2)
                for g in range(2 if l == 0 else 1):
                    key, t = ("Y", l, u, g), 2 * g if l == 0 else 2
                    copy_out(key, y_mix[:, t:t + 2, u * 256:(u + 1) * 256], bank(key).rearrange("p (t n) -> p t n", t=2))
            act.wait_ge(sem(f"act_lo_out{l}"), KT)
            mean_square("post", l, "mix", token_tiles(l, "out"), y_mix_of, lambda t: y_junk[:, :],
                        lambda n: wait_copied(act, key))

        def dense_ffn():
            for j in range(UP_UNITS):
                split_upto(U["up", 0] + j + 2)
                key = ("GU", 0, j, 0)
                wait_filled(act, key)
                if j >= 2:
                    wait_copied(act, ("GU", 0, j - 2, 1))
                act.activation(ffn_sil[:, j % 2, :], bank(key), ACT.Silu).then_inc(emptied[JOBS[key] % BANKS], 1)
            for f in range(FT):
                split_upto(U["down", 0] + f // 2 + 1)
                if f == 0:
                    wait_copied(act, ("GU", 0, FT - 1, 1))
                if f >= 2:
                    act.wait_ge(sem("down_tiles"), f - 1)
                act.activation(ffn_hi[:, f % 2, :], ffnT[:, f, :], ACT.Copy).then_inc(sem("ffn_hi"), 1)
            for t in range(TILES):
                for h in range(2):
                    key = ("D", 0, t, h)
                    copy_out(key, y_ffn[:, t, h * 512:(h + 1) * 512], bank(key))
            mean_square("post", 0, "ffn", range(TILES), y_ffn_of, lambda t: y_junk[:, :], lambda n: wait_copied(act, key))

        for l in range(DEPTH):
            split_upto(U["mod_a", l] + 2)
            norm(l, "mix")
            modulation(l, "a")
            modulated(l, "mix")
            in_projection(l)
            split_upto(U["mod_b", l] + 2)
            attention(l)
            head_std(l, od_std, od_ssq, ("O", l, len(attn_items(l)) - 1))
            gla(l)
            modulation(l, "b")
            merged(l)
            out_projection(l)
            norm(l, "ffn")
            modulated(l, "ffn")
            if l == 0:
                dense_ffn()

        for q in range(4):
            key = ("H2", q)
            wait_filled(act, key)
            act.activation(h2_hi[:, q // 2, (q % 2) * 512:(q % 2 + 1) * 512], bank(key), ACT.Copy).then_inc(sem("h2_hi"), 1)
        act.wait_ge(sem("top_gap"), 1)
        act.activation(rt[:, 4:6], rt[:, 4:6], ACT.Exp).then_inc(sem("top_exp"), 1)
        wait_copied(act, ("POS",))
        with act.Fori(0, EXPERTS) as e:
            many = act.value_load(counts_i[0:1, bass.ds(e, 1)], min_val=0, max_val=LAT) > P
            split_m = [0]

            def split_expert(m_max):
                while split_m[0] <= min(m_max, EXPERT_UNITS - 1):
                    m = split_m[0]
                    n = U["moe", 1] + m
                    act.wait_ge(arrived[n % RING], e * (16 * EXPERT_UNITS // RING) + 16 * (n // RING + 1))
                    wait_expert_unit_used(act, e, m - RING)
                    act.activation(w_hi[:, n % RING, :], raw[:, n % RING, :], ACT.Copy).then_inc(hi_ready, 1)
                    split_m[0] += 1

            def gathered(tau):
                for b in range(2):
                    act.wait_ge(esem("gather", tau), e * 4 + (b + 1))
                    act.activation(xt_hi[:, 4 * b:4 * b + 4, tau, :], psum[:, 4 + b, :].rearrange("p (k n) -> p k n", n=P),
                                   ACT.Copy).then_inc(esem("xt_hi", tau), 1)

            def silu(c, tau):
                act.wait_ge(esem("up", tau), (e + 1) * FC + (c + 1))
                if c:
                    act.wait_ge(esem("act", tau), e * FC + c)
                act.activation(e_sil[:, tau, :], psum[:, up_bank(c, tau), 0:256], ACT.Silu).then_inc(esem("sil", tau), 1)

            def turned(c, tau):
                act.wait_ge(esem("turn", tau), e * FC + (c + 1))
                if c >= 2:
                    act.wait_ge(esem("down", tau), (e + 1) * FC + (c - 1))
                act.activation(eT_hi[:, tau, c % 2, :], psum[:, TURN_BANK, 0:256], ACT.Copy).then_inc(esem("eT_hi", tau), 1)

            def scattered(tau):
                act.wait_ge(esem("selT", tau), e + 1)
                act.activation(selT[:, :, :], psum[:, TURN_BANK, 0:256].rearrange("p (t n) -> p t n", t=2),
                               ACT.Copy).then_inc(esem("selT_copy", tau), 1)
                act.wait_ge(esem("down", tau), (e + 2) * FC)
                if tau:
                    act.wait_ge(esem("scatter", 0), (e + 1) * 4)
                for h in range(2):
                    act.activation(ey_hi[:, h * 512:(h + 1) * 512], psum[:, 4 + 2 * tau + h, :], ACT.Copy).then_inc(
                        esem("ey_hi", tau), 1)

            split_expert(2)
            both(act, many, gathered, [("xt_hi", 2)])
            for c in range(FC + 2):
                here = STEPS[c]
                if "up" in here:
                    split_expert(here["up"][1] + 2)
                    both(act, many, lambda tau: silu(c, tau), [("sil", 1)])
                else:
                    split_expert(EXPERT_UNITS - 1)
                if 1 <= c <= FC:
                    both(act, many, lambda tau: turned(c - 1, tau), [("eT_hi", 1)])
            both(act, many, scattered, [("selT_copy", 1), ("ey_hi", 2)])
        for tau in range(2):
            act.wait_ge(esem("added", tau), EXPERTS * 4 + 1)
        mean_square("post", 1, "ffn", (2, 3), y_moe_of, lambda t: y_junk[:, :], lambda n: None)

    @block.vector
    def _(dve):
        steps = [0]

        def link(ins):
            steps[0] += 1
            ins.then_inc(sem("dve_step"), 1)
            dve.wait_ge(sem("dve_step"), steps[0])

        split = [0]

        def split_upto(n):
            while split[0] <= min(n, U["moe", 1] - 1):
                i = split[0]
                dve.wait_ge(hi_ready, i + 1)
                dve.tensor_tensor(w_lo[:, i % RING, :], raw[:, i % RING, :], w_hi[:, i % RING, :].bitcast(F32),
                                  ALU.subtract).then_inc(lo_ready, 1)
                split[0] += 1

        def empties(ins, key):
            ins.then_inc(emptied[JOBS[key] % BANKS], 1)

        dve.wait_ge(loaded, 64)
        link(dve.tensor_tensor(lam_prod[:, :, :, :], lam_in_sb[:, :, :, 0, :], lam_in_sb[:, :, :, 1, :], ALU.mult))
        dve.tensor_reduce(lam_sum[:, :], lam_prod[:, :, :, :].rearrange("p a b d -> p (a b) d"), X_AXIS,
                          ALU.add).then_inc(sem("lam_sum"), 1)
        dve.wait_ge(sem("lam_exp"), 1)
        for l in range(DEPTH):
            dve.scalar_tensor_tensor(neg_lam[:, l:l + 1], lam_exp[:, 2 * l + 1:2 * l + 2], LAM_INIT[l],
                                     lam_exp[:, 2 * l:2 * l + 1], ALU.subtract, ALU.subtract)
            ins = dve.tensor_scalar(sub_gain[:, l:l + 1], cols[:, V_LAYER + l * V_STRIDE + V_SUB:][:, 0:1],
                                    1.0 - LAM_INIT[l], None, ALU.mult)
        ins.then_inc(sem("lam_ready"), 1)

        def modulation(l, part):
            u0 = U[f"mod_{part}", l] - (0 if part == "a" else MOD_A)
            n = 2 * l + (part == "b")
            dve.wait_ge(sem("c_hi"), 2 * n + 2)
            for i in range(2):
                dve.tensor_tensor(c_cols[:, :, 2 * i + 1], c_act[:, 8 * i:8 * i + 8],
                                  c_cols[:, :, 2 * i].bitcast(F32), ALU.subtract).then_inc(sem("c_lo"), 1)
            for kind, j in mod_steps(part):
                key = (kind, l, j)
                c0 = (j % 4) * 256
                if kind == "mod":
                    split_upto(u0 + j + 2)
                    if is_gate(j):
                        if j == 8:
                            dve.wait_ge(aux_loaded, 16 * (l + 1))
                        c0 += 0 if j < 12 else D_MODEL
                        if j - 2 >= MOD_A:
                            wait_filled(dve, ("modx", l, j - 2))
                        wait_filled(dve, key)
                        empties(dve.tensor_tensor(mod_row_b[:, j % 2, :], bank(key)[0:4, 0:256],
                                                  aux[:, 0, c0:c0 + 256], ALU.add), key)
                        wait_copied(dve, key)
                        dve.tensor_tensor(mod_row_b[:, j % 2, :], mod_row_b[:, j % 2, :], aux[:, 1, c0:c0 + 256],
                                          ALU.mult).then_inc(sem(f"gate_row{l}"), 1)
                elif not is_gate(j):
                    w, s, k = (0 if j < 12 else 1), (j // 4) % 3, 2 * (j % 4)
                    base = V_LAYER + l * V_STRIDE
                    wait_filled(dve, key)
                    dst = modc[:, w, s, k:k + 2, :]
                    bias = cols[:, base + V_BMOD + 2 * j:base + V_BMOD + 2 * j + 2].unsqueeze(2).to_broadcast([P, 2, 2])
                    empties(dve.tensor_tensor(dst, bank(key)[:, 0:4].rearrange("p (k s) -> p k s", k=2), bias,
                                              ALU.add), key)
                    if s == 1:
                        gain = cols[:, base + (V_GPM if w == 0 else V_GPF) + k:][:, 0:2].unsqueeze(2).to_broadcast([P, 2, 2])
                        wait_copied(dve, key)
                        dve.scalar_tensor_tensor(dst, dst, 1.0, gain, ALU.add, ALU.mult).then_inc(sem(f"scale{l}"), 1)

        def norm(l, stage):
            tiles = token_tiles(l, stage)
            dve.wait_ge(sem(f"norm_{stage}{l}"), len(tiles) + 1)
            link(dve.reciprocal(rstd[:, tiles[0]:TILES], std[:, tiles[0]:TILES]))
            for t in tiles:
                dve.tensor_scalar(xn[:, t, :], X[:, t, :], rstd[:, t:t + 1], None, ALU.mult).then_inc(
                    sem(f"xn_{stage}{l}"), 1)

        def low_parts(l, stage, lo):
            for k in range(KT):
                dve.wait_ge(sem(f"act_hi_{stage}{l}"), k + 1)
                dve.tensor_tensor(act_lo[:, k, lo:T], hf[:, k % RING, lo:T], act_hi[:, k, lo:T].bitcast(F32),
                                  ALU.subtract).then_inc(sem(f"act_lo_{stage}{l}"), 1)

        def in_projection(l):
            dve.wait_ge(sem(f"glr_hi{l}"), 1)
            dve.tensor_tensor(glr_lo[:, :, :], wsm[:, l * 256:(l + 1) * 256].rearrange("p (k n) -> p k n", n=32),
                              glr_hi[:, :, :].bitcast(F32), ALU.subtract).then_inc(sem(f"glr_lo{l}"), 1)
            split_upto(U["mod_b", l] - 1)
            key = ("glrT", l)
            wait_filled(dve, key)
            empties(dve.tensor_copy(glrT[0:32, :], bank(key)[0:32, :]), key)

        def rotate(l):
            cos, sin = (rope[:, i:i + 1, :].to_broadcast([P, 2, LAT]) for i in range(2))
            dve.wait_ge(rope_loaded, 16 * (l + 1))
            for b in range(4):
                key = ("rope", l, b)
                dst = (qT if b < 2 else kT)[:, 2 * (b % 2):2 * (b % 2) + 2, CTX:T]
                wait_filled(dve, key)
                empties(dve.tensor_tensor(rope_tmp[:, :, :], bank(key).rearrange("p (h n) -> p h n", h=2), sin,
                                          ALU.mult), key)
                link(dve.tensor_tensor(dst, dst, cos, ALU.mult))
                wait_copied(dve, key)
                dve.tensor_tensor(dst, dst, rope_tmp[:, :, :], ALU.add).then_inc(sem(f"roped{l}"), 1)
                dve.wait_ge(sem(f"roped{l}"), b + 1)

        def attention(l):
            items = attn_items(l)
            n = len(items)
            for i in range(n + 1):
                if i < n:
                    b, keys = i % 2, n_keys(items[i][1])
                    for j in range(2):
                        wait_filled(dve, ("S", l, i, j))
                        ins = dve.tensor_reduce(row_max[:, b, j:j + 1], bank(("S", l, i, j))[:, 0:keys], X_AXIS, ALU.max)
                    link(ins)
                    dve.tensor_scalar(neg_max[:, b, :], row_max[:, b, :], -QK ** -0.5, None, ALU.mult).then_inc(
                        sem(f"neg_max{l}"), 1)
                if i >= 1:
                    b, keys = (i - 1) % 2, n_keys(items[i - 1][1])
                    for j in range(2):
                        wait_copied(dve, ("S", l, i - 1, j))
                    link(dve.reciprocal(row_inv[:, b, :], row_sum[:, b, :]))
                    link(dve.tensor_scalar(row_inv[:, b, 1:2], row_inv[:, b, 1:2], neg_lam[:, l:l + 1], None, ALU.mult))
                    link(dve.tensor_scalar(probs[:, b, 1, 0:keys], probs[:, b, 1, 0:keys], row_inv[:, b, 1:2], None,
                                           ALU.mult))
                    dve.scalar_tensor_tensor(probs[:, b, 0, 0:keys], probs[:, b, 0, 0:keys], row_inv[:, b, 0:1],
                                             probs[:, b, 1, 0:keys], ALU.mult, ALU.add).then_inc(sem(f"probs{l}"), 1)
            heads_normed(l, od, od_std, od_rstd, 1)

        def heads_normed(l, dst, s, r, count):
            t0 = token_tiles(l, "out")[0]
            dve.wait_ge(sem(f"head_std{l}"), count)
            link(dve.reciprocal(r[:, 4 * t0:16], s[:, 4 * t0:16]))
            part = dst[:, t0:TILES, :].rearrange("p t (h n) -> p (t h) n", n=P)
            dve.tensor_tensor(part, part, r[:, 4 * t0:16].unsqueeze(2).to_broadcast([P, 16 - 4 * t0, P]),
                              ALU.mult).then_inc(sem(f"merged{l}"), 1)

        def gla(l):
            wait_copied(dve, ("O", l, len(attn_items(l)) - 1))
            for t in range(TILES):
                key = ("Z", l, t)
                dve.wait_ge(sem(f"zabs{l}"), t + 1)
                empties(dve.tensor_scalar(gl[:, t, :], bank(key), 0.0, None, ALU.min), key)
            for t in range(TILES):
                wait_copied(dve, ("Z", l, t))
                dve.wait_ge(sem(f"gate_log{l}"), TILES + t + 1)
                dve.tensor_tensor(gl[:, t, :], gl[:, t, :], zabs[:, t, :], ALU.subtract).then_inc(sem(f"gl{l}"), 1)
            last_of, mid_of = (CHUNK - 1, 0), (CHUNK // 2 - 1, CHUNK // 2)
            view = lambda a: a.rearrange("p (c n) -> p c n", n=CHUNK)
            for dp in range(4):
                d = dp // 2
                wait_copied(dve, ("G", l, dp))
                g = view(GT[:, dp, :])
                at_chunk = lambda i: g[:, :, i:i + 1].to_broadcast([P, T // CHUNK, CHUNK])
                dve.tensor_tensor(view(gexp[:, 0, dp, :]), g, at_chunk(mid_of[d]), ALU.subtract).then_inc(sem(f"gsub{l}"), 1)
                dve.tensor_tensor(view(gexp[:, 2, dp, :]), at_chunk(last_of[d]), g, ALU.subtract).then_inc(sem(f"gsub{l}"), 1)
            for dp in range(4):
                d, pair = divmod(dp, 2)
                dve.wait_ge(sem(f"gexp{l}"), 4 * dp + 4)
                link(dve.tensor_copy(decay[:, dp, :], view(gexp[:, 3, dp, :])[:, :, last_of[d]]))
                for kind, other in ((2, gkT), (0, gqT), (1, gkT), (3, gqT)):
                    dve.tensor_tensor(gexp[:, kind, dp, :], gexp[:, kind, dp, :], other[:, pair, :],
                                      ALU.mult).then_inc(sem(f"gmul{l}"), 1)
            for dp in range(4):
                order = chunk_order(dp // 2)
                for n in range(7):
                    here, after = order[n], order[n + 1]
                    key = ("DS", l, dp, here % 2)
                    ds = bank(key)[:, (here // 2) * P:(here // 2 + 1) * P]
                    if n < 2:
                        wait_filled(dve, key)
                    if n == 0:
                        ins = dve.tensor_copy(states[:, dp, after, :], ds)
                    else:
                        ins = dve.scalar_tensor_tensor(states[:, dp, after, :], states[:, dp, here, :],
                                                       decay[:, dp, here:here + 1], ds, ALU.mult, ALU.add)
                    if n in (5, 6):
                        empties(ins, key)
                        wait_copied(dve, key)
                    else:
                        link(ins)
            for i, (h, t) in enumerate(gla_items(l)):
                key = ("M", l, i)
                wait_filled(dve, key)
                if i >= 2:
                    wait_filled(dve, ("OG", l, i - 2))
                elif l == 0:
                    dve.wait_ge(sem("zeros"), 2)
                elif i < 2:
                    wait_filled(dve, ("OG", 0, len(gla_items(0)) - 1))
                empties(dve.copy_predicated(Am[:, i % 2, :, :].rearrange("p d n -> p (d n)"), tri.bitcast(I32),
                                            bank(key)[:, 0:2 * P]), key)
            t0 = token_tiles(l, "out")[0]
            dve.wait_ge(sem(f"gg_silu{l}"), 1)
            wait_copied(dve, ("OG", l, len(gla_items(l)) - 1))
            link(dve.tensor_tensor(og[:, t0:TILES, :], og[:, t0:TILES, :], gg[:, t0:TILES, :], ALU.mult))
            heads_normed(l, og, og_std, og_rstd, 2)

        def residual(l, stage, y):
            tiles = token_tiles(l, "out")
            dve.wait_ge(sem(f"post_{stage}{l}"), len(tiles) + 1)
            link(dve.reciprocal(rstd[:, tiles[0]:TILES], std[:, tiles[0]:TILES]))
            w = 0 if stage == "mix" else 1
            for j in range(8, 12) if w == 0 else range(20, 24):
                wait_copied(dve, ("modx", l, j))
            for t in tiles:
                link(dve.scalar_tensor_tensor(y(t), y(t), rstd[:, t:t + 1],
                                              gate[:, w, 0 if t < 2 else 1, :], ALU.mult, ALU.mult))
                dve.tensor_tensor(X[:, t, :], X[:, t, :], y(t), ALU.add).then_inc(sem(f"x_{stage}{l}"), 1)

        def dense_ffn():
            for j in range(UP_UNITS):
                split_upto(U["up", 0] + j + 2)
                wait_copied(dve, ("GU", 0, j, 0))
                key = ("GU", 0, j, 1)
                wait_filled(dve, key)
                empties(dve.tensor_tensor(ffnT[:, j, :], ffn_sil[:, j % 2, :], bank(key), ALU.mult), key)
            for f in range(FT):
                split_upto(U["down", 0] + f // 2 + 1)
                dve.wait_ge(sem("ffn_hi"), f + 1)
                dve.tensor_tensor(ffn_lo[:, f % 2, :], ffnT[:, f, :], ffn_hi[:, f % 2, :].bitcast(F32),
                                  ALU.subtract).then_inc(sem("ffn_lo"), 1)

        for l in range(DEPTH):
            split_upto(U["mod_a", l] + 2)
            norm(l, "mix")
            modulation(l, "a")
            low_parts(l, "mix", 0)
            in_projection(l)
            split_upto(U["mod_b", l] + 2)
            rotate(l)
            attention(l)
            gla(l)
            modulation(l, "b")
            low_parts(l, "out", token_tiles(l, "out")[0] * P)
            split_upto(U["out", l] + OUT_UNITS - 1)
            residual(l, "mix", y_mix_of)
            norm(l, "ffn")
            if l == 0:
                low_parts(l, "ffn", 0)
                dense_ffn()
                residual(l, "ffn", y_ffn_of)

        for q in range(4):
            key = ("H2", q)
            part = slice((q % 2) * 512, (q % 2 + 1) * 512)
            dve.wait_ge(sem("h2_hi"), q + 1)
            empties(dve.tensor_tensor(h2_lo[:, q // 2, part], bank(key), h2_hi[:, q // 2, part].bitcast(F32),
                                      ALU.subtract), key)
        link(dve.memset(y_moe[:, :, :], 0.0))
        field = lambda i: route[:, :, i, :]
        two = lambda i: rt[:, 2 * i:2 * i + 2]
        wide = lambda a: a.unsqueeze(2).to_broadcast([P, 2, EXPERTS])
        LOGIT, FIRST, SECOND, TAKEN, POSITION, WEIGHT = range(6)
        descending = const[:, C_DESC:C_DESC + EXPERTS].unsqueeze(1).to_broadcast([P, 2, EXPERTS])
        key = ("LG",)
        wait_filled(dve, key)
        empties(dve.tensor_copy(field(LOGIT), bank(key)[:, 0:2 * EXPERTS].rearrange("p (t e) -> p t e", t=2)), key)
        wait_copied(dve, key)
        for n, pick in enumerate((FIRST, SECOND)):
            link(dve.tensor_reduce(two(n), field(LOGIT), X_AXIS, ALU.max))
            link(dve.tensor_tensor(field(pick), field(LOGIT), wide(two(n)), ALU.is_equal))
            link(dve.tensor_tensor(field(pick), field(pick), descending, ALU.mult))
            link(dve.tensor_reduce(two(3), field(pick), X_AXIS, ALU.max))
            link(dve.tensor_tensor(field(pick), field(pick), wide(two(3)), ALU.is_equal))
            if n == 0:
                link(dve.scalar_tensor_tensor(field(LOGIT), field(FIRST), -3.0e38, field(LOGIT), ALU.mult, ALU.add))
        dve.tensor_tensor(two(2), two(1), two(0), ALU.subtract).then_inc(sem("top_gap"), 1)
        dve.tensor_tensor(field(TAKEN), field(FIRST), field(SECOND), ALU.add).then_inc(sem("taken"), 1)
        dve.wait_ge(sem("top_exp"), 1)
        link(dve.tensor_scalar(two(4), two(2), 1.0, None, ALU.add))
        link(dve.reciprocal(two(4), two(4)))
        link(dve.tensor_tensor(two(5), two(4), two(2), ALU.mult))
        link(dve.tensor_tensor(field(FIRST), field(FIRST), wide(two(4)), ALU.mult))
        link(dve.tensor_tensor(field(SECOND), field(SECOND), wide(two(5)), ALU.mult))
        link(dve.tensor_tensor(field(WEIGHT), field(FIRST), field(SECOND), ALU.add))
        key = ("POS",)
        wait_filled(dve, key)
        dve.tensor_copy(field(POSITION), bank(key)[:, 0:2 * EXPERTS].rearrange("p (t e) -> p t e", t=2))
        empties(dve.tensor_copy(counts_i[:, :], bank(key)[:, 2 * EXPERTS:3 * EXPERTS]), key)
        wait_copied(dve, key)
        for tau in range(2):
            dve.sem_inc(esem("added", tau), 1)

        with dve.Fori(0, EXPERTS) as e:
            many = dve.value_load(counts_i[0:1, bass.ds(e, 1)], min_val=0, max_val=LAT) > P
            split_m = [0]

            def split_expert(m_max):
                while split_m[0] <= min(m_max, EXPERT_UNITS - 1):
                    n = U["moe", 1] + split_m[0]
                    dve.wait_ge(hi_ready, e * EXPERT_UNITS + (n + 1))
                    dve.tensor_tensor(w_lo[:, n % RING, :], raw[:, n % RING, :], w_hi[:, n % RING, :].bitcast(F32),
                                      ALU.subtract).then_inc(lo_ready, 1)
                    split_m[0] += 1

            def gathered(tau):
                for b in range(2):
                    dve.wait_ge(esem("gather", tau), e * 4 + (b + 3))
                    dve.tensor_copy(xt_lo[:, 4 * b:4 * b + 4, tau, :],
                                    psum[:, 6 + b, :].rearrange("p (k n) -> p k n", n=P)).then_inc(esem("xt_lo", tau), 1)

            def product(c, tau):
                dve.wait_ge(esem("sil", tau), e * FC + (c + 1))
                if c >= 2:
                    dve.wait_ge(esem("turn", tau), e * FC + (c - 1))
                dve.tensor_tensor(e_act[:, tau, c % 2, :], e_sil[:, tau, :], psum[:, up_bank(c, tau), 256:512],
                                  ALU.mult).then_inc(esem("act", tau), 1)

            def turned(c, tau):
                dve.wait_ge(esem("eT_hi", tau), e * FC + (c + 1))
                dve.tensor_tensor(eT_lo[:, tau, c % 2, :], psum[:, TURN_BANK, 0:256],
                                  eT_hi[:, tau, c % 2, :].bitcast(F32), ALU.subtract).then_inc(esem("eT_lo", tau), 1)

            def scattered(tau):
                for h in range(2):
                    dve.wait_ge(esem("ey_hi", tau), e * 2 + (h + 1))
                    part = slice(h * 512, (h + 1) * 512)
                    dve.tensor_tensor(ey_lo[:, part], psum[:, 4 + 2 * tau + h, :], ey_hi[:, part].bitcast(F32),
                                      ALU.subtract).then_inc(esem("ey_lo", tau), 1)
                for n in range(4):
                    tt, part = n // 2, slice((n % 2) * 512, (n % 2 + 1) * 512)
                    dve.wait_ge(esem("scatter", tau), e * 4 + (n + 1))
                    if tau:
                        dve.wait_ge(esem("added", 0), e * 4 + (n + 2))
                    dve.scalar_tensor_tensor(y_moe[:, tt, part], psum[:, n % 2, :], e_cols[:, 3 * tt + 2:3 * tt + 3],
                                             y_moe[:, tt, part], ALU.mult, ALU.add).then_inc(esem("added", tau), 1)

            for tau in range(2):
                dve.wait_ge(esem("added", tau), e * 4 + 1)
            dve.tensor_copy(e_cols[:, :].rearrange("p (t f) -> p t f", t=2),
                            route[:, :, 3:6, bass.ds(e, 1)].rearrange("p t f a -> p t (f a)")).then_inc(sem("e_cols"), 1)
            dve.wait_ge(sem("e_cols"), e + 1)
            for tt in range(2):
                dve.tensor_scalar(sel[:, tt, :], const[:, C_IOTA:C_IOTA + 2 * P], e_cols[:, 3 * tt + 1:3 * tt + 2],
                                  e_cols[:, 3 * tt:3 * tt + 1], ALU.is_equal, ALU.mult).then_inc(sem("sel"), 1)
            split_expert(2)
            both(dve, many, gathered, [("xt_lo", 2)])
            for c in range(FC + 2):
                here = STEPS[c]
                if "up" in here:
                    split_expert(here["up"][1] + 2)
                    both(dve, many, lambda tau: product(c, tau), [("act", 1)])
                else:
                    split_expert(EXPERT_UNITS - 1)
                if 1 <= c <= FC:
                    both(dve, many, lambda tau: turned(c - 1, tau), [("eT_lo", 1)])
            both(dve, many, scattered, [("ey_lo", 2), ("added", 4)])
        for tau in range(2):
            dve.wait_ge(esem("added", tau), EXPERTS * 4 + 1)
        residual(1, "ffn", y_moe_of)

    @block.tensor
    def _(pe):
        pe.wait_ge(loaded, 64)

        def three(dst, lhs, rhs, first, last):
            for n, (a, b) in enumerate(PASSES):
                ins = pe.matmul(dst, lhs(a), rhs(b), start=first and n == 0, stop=last and n == 2)
            return ins

        def unit(n):
            pe.wait_ge(lo_ready, n + 1)
            return n % RING

        def modulation(l, part):
            u0 = U[f"mod_{part}", l] - (0 if part == "a" else MOD_A)
            row = mod_row if part == "a" else mod_row_b
            pe.wait_ge(sem("c_lo"), 2 * (2 * l + (part == "b")) + 2)
            gates = 0
            for kind, j in mod_steps(part):
                key = (kind, l, j)
                if kind == "mod":
                    s = unit(u0 + j)
                    wait_emptied(pe, key)
                    for k in range(KT):
                        for part_of in range(2):
                            ins = pe.matmul(bank(key)[:, 0:256], c_cols[:, k, :], weights[part_of][:, s, k * 256:(k + 1) * 256],
                                            start=k == 0 and part_of == 0, stop=k == KT - 1 and part_of == 1)
                elif is_gate(j):
                    gates += 1
                    pe.wait_ge(sem(f"gate_row{l}"), gates)
                    wait_emptied(pe, key)
                    for i in range(2):
                        ins = pe.matmul(bank(key)[:, i * 256:(i + 1) * 256], const[0:4, C_SELB + i * P:C_SELB + (i + 1) * P],
                                        row[:, j % 2, :], start=True, stop=True)
                else:
                    wait_copied(pe, ("mod", l, j))
                    wait_emptied(pe, key)
                    for i in range(2):
                        ins = pe.matmul(bank(key)[:, 2 * i:2 * i + 2], row[:, j % 2, i * P:(i + 1) * P],
                                        const[0:4, C_SELC:C_SELC + 2], start=True, stop=True)
                ins.then_inc(filled, 1)

        def turn(l, stage):
            tiles = token_tiles(l, stage)
            pe.wait_ge(sem(f"xn_{stage}{l}"), len(tiles))
            for k in range(KT):
                key = ("T", l, stage, k)
                wait_emptied(pe, key)
                for t in tiles:
                    ins = pe.transpose(bank(key)[:, t * P:(t + 1) * P], xn[:, t, k * P:(k + 1) * P], ident)
                ins.then_inc(filled, 1)

        def in_projection(l):
            for u in range(IN_F):
                s = unit(U["in", l] + u)
                for i in range(2):
                    key = ("F", l, 2 * u + i)
                    wait_emptied(pe, key)
                    for k in range(KT):
                        pe.wait_ge(sem(f"act_lo_mix{l}"), k + 1)
                        ins = three(bank(key), lambda a: weights[a][:, s, k * 256 + i * P:k * 256 + (i + 1) * P],
                                    lambda b: acts[b][:, k, :], k == 0, k == KT - 1)
                    ins.then_inc(filled, 1)
            for u in range(IN_K):
                s = unit(U["in", l] + IN_F + u)
                for g in range(2):
                    key = ("K", l, u, g)
                    wait_emptied(pe, key)
                    for i in range(2):
                        for k in range(KT):
                            ins = three(bank(key)[:, i * 256:(i + 1) * 256],
                                        lambda a: acts[a][:, k, (2 * g + i) * P:(2 * g + i + 1) * P],
                                        lambda b: weights[b][:, s, k * 256:(k + 1) * 256], k == 0, k == KT - 1)
                    ins.then_inc(filled, 1)
            key = ("glr", l)
            pe.wait_ge(sem(f"glr_lo{l}"), 1)
            wait_emptied(pe, key)
            for t in range(TILES):
                for k in range(KT):
                    ins = three(bank(key)[:, t * 32:(t + 1) * 32], lambda a: acts[a][:, k, t * P:(t + 1) * P],
                                lambda b: (glr_hi, glr_lo)[b][:, k, :], k == 0, k == KT - 1)
            ins.then_inc(filled, 1)
            key = ("glrT", l)
            wait_copied(pe, ("glr", l))
            wait_emptied(pe, key)
            for t in range(TILES):
                ins = pe.transpose(bank(key)[0:32, t * P:(t + 1) * P], glr_tok[:, t, :], ident)
            ins.then_inc(filled, 1)

        def rotate(l):
            for b in range(4):
                key = ("rope", l, b)
                src = qT if b < 2 else kT
                wait_emptied(pe, key)
                for i in range(2):
                    h = 2 * (b % 2) + i
                    wait_copied(pe, ("F", l, h + (0 if b < 2 else 4)))
                    ins = pe.matmul(bank(key)[:, i * 256:(i + 1) * 256], const[:, C_PERM:C_PERM + P], src[:, h, CTX:T],
                                    start=True, stop=True)
                ins.then_inc(filled, 1)

        def attention(l):
            items = attn_items(l)
            n = len(items)
            pe.wait_ge(sem(f"roped{l}"), 4)
            for g in range(2):
                for u in range(2):
                    wait_copied(pe, ("K", l, u, g))
            for i in range(n + 2):
                if i < n:
                    h, t = items[i]
                    keys = n_keys(t)
                    for j in range(2):
                        key = ("S", l, i, j)
                        wait_emptied(pe, key)
                        r = slice(j * QK, (j + 1) * QK)
                        pe.matmul(bank(key)[:, 0:keys], qT[r, h, t * P:(t + 1) * P], kT[r, h, 0:keys], start=True,
                                  stop=True).then_inc(filled, 1)
                if 1 <= i <= n:
                    key, keys = ("PT", l, i - 1), n_keys(items[i - 1][1])
                    pe.wait_ge(sem(f"probs{l}"), i)
                    wait_emptied(pe, key)
                    for k in range(keys // P):
                        ins = pe.transpose(bank(key)[:, k * P:(k + 1) * P], probs[:, (i - 1) % 2, 0, k * P:(k + 1) * P], ident)
                    ins.then_inc(filled, 1)
                if i >= 2:
                    key, (h, t) = ("O", l, i - 2), items[i - 2]
                    wait_copied(pe, ("PT", l, i - 2))
                    wait_emptied(pe, key)
                    tiles = n_keys(t) // P
                    for k in range(tiles):
                        ins = pe.matmul(bank(key)[:, 0:P], probsT[:, i % 2, k * P:(k + 1) * P], v[:, k, h * P:(h + 1) * P],
                                        start=k == 0, stop=k == tiles - 1)
                    ins.then_inc(filled, 1)

        def gla(l):
            wait_copied(pe, ("glrT", l))
            pe.wait_ge(gw2_loaded, 16 * (l + 1))
            pe.wait_ge(sem("zeros"), 2)
            for t in range(TILES):
                key = ("Z", l, t)
                wait_emptied(pe, key)
                pe.matmul(bank(key), glrT[0:33, t * P:(t + 1) * P], gw2[0:33, :], start=True, stop=True).then_inc(filled, 1)
            pe.wait_ge(sem(f"gl{l}"), TILES)
            for dp in range(4):
                key, d = ("G", l, dp), dp // 2
                wait_emptied(pe, key)
                for t in range(TILES):
                    ins = pe.matmul(bank(key)[:, t * P:(t + 1) * P], gl[:, t, dp * P:(dp + 1) * P],
                                    const[:, C_TRI + d * P:C_TRI + (d + 1) * P], start=True, stop=True)
                ins.then_inc(filled, 1)
            for u in range(2, 4):
                for g in range(2):
                    wait_copied(pe, ("K", l, u, g))
            for dp in range(4):
                pair = dp % 2
                key = ("KT", l, dp)
                pe.wait_ge(sem(f"gmul{l}"), 4 * dp + 1)
                wait_emptied(pe, key)
                for t in range(TILES):
                    ins = pe.transpose(bank(key)[:, t * P:(t + 1) * P], gexp[:, 2, dp, t * P:(t + 1) * P], ident)
                ins.then_inc(filled, 1)
                wait_copied(pe, key)
                for half in range(2):
                    key = ("DS", l, dp, half)
                    wait_emptied(pe, key)
                    r = slice(half * CHUNK, (half + 1) * CHUNK)
                    for t in range(TILES):
                        for hh in range(2):
                            ins = pe.matmul(bank(key)[hh * QK:(hh + 1) * QK, t * P:(t + 1) * P],
                                            klT[r, dp, t, hh * QK:(hh + 1) * QK],
                                            gv[r, t, (2 * pair + hh) * P:(2 * pair + hh + 1) * P], start=True, stop=True)
                    ins.then_inc(filled, 1)
            pe.wait_ge(sem(f"gmul{l}"), 16)
            items = gla_items(l)
            for i in range(len(items) + 1):
                if i < len(items):
                    h, t = items[i]
                    pair, r = h // 2, slice((h % 2) * QK, (h % 2 + 1) * QK)
                    key = ("M", l, i)
                    wait_emptied(pe, key)
                    for d in range(2):
                        dp = 2 * d + pair
                        ins = pe.matmul(bank(key)[:, d * P:(d + 1) * P], gexp[r, 1, dp, t * P:(t + 1) * P],
                                        gexp[r, 0, dp, t * P:(t + 1) * P], start=True, stop=True)
                    ins.then_inc(filled, 1)
                if i >= 1:
                    h, t = items[i - 1]
                    pair, r = h // 2, slice((h % 2) * QK, (h % 2 + 1) * QK)
                    key = ("OG", l, i - 1)
                    wait_copied(pe, ("M", l, i - 1))
                    if i == 1:
                        for dp in range(4):
                            for half in range(2):
                                wait_copied(pe, ("DS", l, dp, half))
                    wait_emptied(pe, key)
                    for d in range(2):
                        pe.matmul(bank(key)[:, 0:P], Am[:, (i - 1) % 2, d, :], gv[:, t, h * P:(h + 1) * P],
                                  start=d == 0, stop=False, skip_group_check=True)
                    parts = [(half, d) for half in range(2) for d in range(2)
                             if 2 * t + half != chunk_order(d)[0]]
                    for n, (half, d) in enumerate(parts):
                        c = 2 * t + half
                        ins = pe.matmul(bank(key)[half * CHUNK:(half + 1) * CHUNK, 0:P],
                                        gexp[r, 3, 2 * d + pair, c * CHUNK:(c + 1) * CHUNK], states[r, 2 * d + pair, c, :],
                                        start=False, stop=n == len(parts) - 1, skip_group_check=True)
                    ins.then_inc(filled, 1)

        def out_projection(l):
            tiles = token_tiles(l, "out")
            pe.wait_ge(sem(f"merged{l}"), 2)
            for f in range(KT):
                key = ("MT", l, f)
                src = od if f < 4 else og
                wait_emptied(pe, key)
                for t in tiles:
                    ins = pe.transpose(bank(key)[:, t * P:(t + 1) * P], src[:, t, (f % 4) * P:(f % 4 + 1) * P], ident)
                ins.then_inc(filled, 1)
            for u in range(OUT_UNITS):
                s = unit(U["out", l] + u)
                for g in range(2 if l == 0 else 1):
                    key = ("Y", l, u, g)
                    wait_emptied(pe, key)
                    for i in range(2):
                        t = (2 * g if l == 0 else 2) + i
                        for k in range(KT):
                            pe.wait_ge(sem(f"act_lo_out{l}"), k + 1)
                            ins = three(bank(key)[:, i * 256:(i + 1) * 256], lambda a: acts[a][:, k, t * P:(t + 1) * P],
                                        lambda b: weights[b][:, s, k * 256:(k + 1) * 256], k == 0, k == KT - 1)
                    ins.then_inc(filled, 1)

        def dense_ffn():
            for j in range(UP_UNITS):
                s = unit(U["up", 0] + j)
                for i in range(2):
                    key = ("GU", 0, j, i)
                    wait_emptied(pe, key)
                    for k in range(KT):
                        if j == 0 and i == 0:
                            pe.wait_ge(sem("act_lo_ffn0"), k + 1)
                        ins = three(bank(key), lambda a: weights[a][:, s, k * 256 + i * P:k * 256 + (i + 1) * P],
                                    lambda b: acts[b][:, k, :], k == 0, k == KT - 1)
                    ins.then_inc(filled, 1)
            for t in range(TILES):
                for h in range(2):
                    wait_emptied(pe, ("D", 0, t, h))
            for f in range(FT):
                s = unit(U["down", 0] + f // 2)
                pe.wait_ge(sem("ffn_lo"), f + 1)
                for t in range(TILES):
                    for h in range(2):
                        c0 = (f % 2) * D_MODEL + h * 512
                        ins = three(bank(("D", 0, t, h)), lambda a: (ffn_hi, ffn_lo)[a][:, f % 2, t * P:(t + 1) * P],
                                    lambda b: weights[b][:, s, c0:c0 + 512], f == 0, f == FT - 1)
                        if f == FT - 1:
                            ins.then_inc(filled, 1)
                if f < FT - 1:
                    ins.then_inc(sem("down_tiles"), 1)

        for l in range(DEPTH):
            modulation(l, "a")
            turn(l, "mix")
            in_projection(l)
            rotate(l)
            attention(l)
            gla(l)
            modulation(l, "b")
            out_projection(l)
            turn(l, "ffn")
            if l == 0:
                dense_ffn()

        for q in range(4):
            key, tt = ("H2", q), q // 2
            wait_emptied(pe, key)
            for k in range(4):
                kk = 4 * (q % 2) + k
                wait_copied(pe, ("T", 1, "ffn", kk))
                ins = pe.transpose(bank(key)[:, k * P:(k + 1) * P], h2T[:, kk, tt * P:(tt + 1) * P], ident)
            ins.then_inc(filled, 1)
        key = ("LG",)
        wait_emptied(pe, key)
        for tt in range(2):
            for k in range(KT):
                ins = pe.matmul(bank(key)[:, tt * EXPERTS:(tt + 1) * EXPERTS], h2T[:, k, tt * P:(tt + 1) * P],
                                wsm[:, 512 + k * EXPERTS:512 + (k + 1) * EXPERTS], start=k == 0, stop=k == KT - 1)
        ins.then_inc(filled, 1)
        key = ("POS",)
        pe.wait_ge(sem("taken"), 1)
        wait_emptied(pe, key)
        upper = const[:, C_UPPER:C_UPPER + P]
        for field_at, parts in ((0, ((upper, 0),)), (1, ((ones, 0), (upper, 1))), (2, ((ones, 0), (ones, 1)))):
            for n, (lhs, tt) in enumerate(parts):
                ins = pe.matmul(bank(key)[:, field_at * EXPERTS:(field_at + 1) * EXPERTS], lhs, route[:, tt, 3, :],
                                start=n == 0, stop=n == len(parts) - 1)
        ins.then_inc(filled, 1)
        wait_copied(pe, ("POS",))
        for tau in range(2):
            for name in ("half", "up", "down"):
                pe.sem_inc(esem(name, tau), FC)

        with pe.Fori(0, EXPERTS) as e:
            many = pe.value_load(counts_i[0:1, bass.ds(e, 1)], min_val=0, max_val=LAT) > P

            def eunit(m):
                n = U["moe", 1] + m
                pe.wait_ge(lo_ready, e * EXPERT_UNITS + (n + 1))
                return n % RING

            def gather(tau):
                if tau:
                    pe.wait_ge(esem("xt_hi", 0), e * 2 + 2)
                    pe.wait_ge(esem("xt_lo", 0), e * 2 + 2)
                for n in range(4):
                    src = (h2_hi, h2_lo)[n // 2]
                    for k in range(4):
                        kk = 4 * (n % 2) + k
                        for tt in range(2):
                            ins = pe.matmul(psum[:, 4 + n, k * P:(k + 1) * P], src[:, tt, kk * P:(kk + 1) * P],
                                            sel[:, tt, tau * P:(tau + 1) * P], start=tt == 0, stop=tt == 1)
                    ins.then_inc(esem("gather", tau), 1)

            def up(c, half, s, tau):
                if half == 0:
                    if c == 0:
                        pe.wait_ge(esem("xt_hi", tau), e * 2 + 2)
                        pe.wait_ge(esem("xt_lo", tau), e * 2 + 2)
                    if tau == 0 and c < 2:
                        for i in range(2):
                            pe.wait_ge(esem("added", i), e * 4 + 1)
                    elif tau == 0:
                        pe.wait_ge(esem("act", 0), e * FC + (c - 1))
                    elif c:
                        pe.wait_ge(esem("act", 1), e * FC + c)
                for kk in range(4):
                    k = 4 * half + kk
                    ins = three(psum[:, up_bank(c, tau), :], lambda a: (xt_hi, xt_lo)[a][:, k, tau, :],
                                lambda b: weights[b][:, s, kk * 512:(kk + 1) * 512], k == 0, k == KT - 1)
                ins.then_inc(esem(("half", "up")[half], tau), 1)

            def turned(c, tau):
                pe.wait_ge(esem("act", tau), e * FC + (c + 1))
                if tau:
                    pe.wait_ge(esem("eT_lo", 0), e * FC + (c + 1))
                elif c:
                    for i in range(2):
                        pe.wait_ge(esem("eT_lo", i), e * FC + c)
                for j in range(2):
                    ins = pe.transpose(psum[:, TURN_BANK, j * P:(j + 1) * P], e_act[:, tau, c % 2, j * P:(j + 1) * P], ident)
                ins.then_inc(esem("turn", tau), 1)

            def down(c, s, tau):
                pe.wait_ge(esem("eT_lo", tau), e * FC + (c + 1))
                for j in range(2):
                    for h in range(2):
                        ins = three(psum[:, 4 + 2 * tau + h, :],
                                    lambda a: (eT_hi, eT_lo)[a][:, tau, c % 2, j * P:(j + 1) * P],
                                    lambda b: weights[b][:, s, j * D_MODEL + h * 512:j * D_MODEL + (h + 1) * 512],
                                    c == 0 and j == 0, c == FC - 1 and j == 1)
                ins.then_inc(esem("down", tau), 1)

            def scatter(tau):
                if tau:
                    pass
                for tt in range(2):
                    ins = pe.transpose(psum[:, TURN_BANK, tt * P:(tt + 1) * P],
                                       sel[:, tt, tau * P:(tau + 1) * P].bitcast(F32), ident)
                ins.then_inc(esem("selT", tau), 1)
                pe.wait_ge(esem("selT_copy", tau), e + 1)
                for n in range(4):
                    tt, h = divmod(n, 2)
                    if n < 2:
                        pe.wait_ge(esem("ey_lo", tau), e * 2 + (h + 1))
                    if n >= 2:
                        pe.wait_ge(esem("added", tau), e * 4 + n)
                    elif tau:
                        pe.wait_ge(esem("added", 0), e * 4 + 5)
                    for i, src in enumerate((ey_hi, ey_lo)):
                        ins = pe.matmul(psum[:, n % 2, :], selT[:, tt, :], src[:, h * 512:(h + 1) * 512],
                                        start=i == 0, stop=i == 1)
                    ins.then_inc(esem("scatter", tau), 1)

            pe.wait_ge(sem("sel"), e * 2 + 2)
            both(pe, many, gather, [("gather", 4)])
            for c in range(FC + 2):
                here = STEPS[c]
                if "up" in here:
                    for half in range(2):
                        s = eunit(here["up"][half])
                        both(pe, many, lambda tau: up(c, half, s, tau), [(("half", "up")[half], 1)])
                if 1 <= c <= FC:
                    both(pe, many, lambda tau: turned(c - 1, tau), [("turn", 1)])
                if "down" in here:
                    s = eunit(here["down"])
                    both(pe, many, lambda tau: down(c - 2, s, tau), [("down", 1)])
            for i in range(2):
                pe.wait_ge(esem("eT_lo", i), (e + 1) * FC)
            both(pe, many, scatter, [("selT", 1), ("scatter", 4)])


def constants():
    import numpy as np
    c = np.zeros((P, N_CONST), np.float32)
    i = np.arange(P)
    c[:, C_IDENT:C_IDENT + P] = np.eye(P)
    same = (i[:, None] // CHUNK) == (i[None, :] // CHUNK)
    c[:, C_TRI:C_TRI + P] = (same & (i[:, None] <= i[None, :])) / 16.0
    c[:, C_TRI + P:C_TRI + 2 * P] = (same & (i[:, None] >= i[None, :])) / 16.0
    c[:, C_UPPER:C_UPPER + P] = i[:, None] < i[None, :]
    c[:, C_ONES:C_ONES + P] = 1.0
    partner = np.where(i % 32 < 16, i + 16, i - 16)
    c[partner, C_PERM + i] = 1.0
    c[:, C_IOTA:C_IOTA + 2 * P] = np.arange(2 * P)
    c[2:4, C_SELB:C_SELB + P] = 1.0
    c[0:2, C_SELB + P:C_SELB + 2 * P] = 1.0
    c[2:4, C_SELC] = 1.0
    c[0:2, C_SELC + 1] = 1.0
    c[:, C_EPS] = EPS
    c[:, C_DESC:C_DESC + EXPERTS] = np.arange(EXPERTS, 0, -1)
    return c


def rope_constants():
    import numpy as np
    n_freq = QK // 4
    inv = (np.float32(ROPE_THETA) ** (-np.arange(n_freq, dtype=np.float32) / np.float32(n_freq))).astype(np.float32)
    token, feature = np.arange(LAT), np.arange(P)
    place = np.where((feature[:, None] % QK) < QK // 2, token // GRID_W, token % GRID_W).astype(np.float32)
    angle = place * inv[feature % n_freq][:, None]
    sign = np.where(feature % 32 < 16, -1.0, 1.0).astype(np.float32)[:, None]
    return np.ascontiguousarray(np.stack([np.cos(angle), np.sin(angle) * sign], 1).astype(np.float32))


def pack(inputs):
    import numpy as np
    a = {k: np.asarray(x) for k, x in inputs.items()}

    def by_rows(w):
        return w.reshape(KT, P, 256).transpose(1, 0, 2).reshape(P, UNIT)

    units = np.empty((N_UNITS, P, UNIT), np.float32)
    n = 0

    def put(w):
        nonlocal n
        units[n] = w
        n += 1

    for l in range(DEPTH):
        mod, w_in = a["w_mod"][l], a["w_in"][l]
        order = [0, 256, 512, 768, 1536, 1792, 1024, 1280, 2048, 2304, 2560, 2816]
        for j in range(MOD_A):
            put(by_rows(mod[:, j * 256:(j + 1) * 256]))
        for c in order:
            put(by_rows(w_in[:, c:c + 256]))
        for j in range(MOD_A, MOD_UNITS):
            put(by_rows(mod[:, j * 256:(j + 1) * 256]))
        for u in range(OUT_UNITS):
            put(by_rows(a["w_out"][l][:, u * 256:(u + 1) * 256]))
        if l == 0:
            for j in range(UP_UNITS):
                put(by_rows(np.concatenate([a[w][0][:, j * P:(j + 1) * P] for w in ("ffn_w1", "ffn_w3")], 1)))
            for i in range(DOWN_UNITS):
                put(a["ffn_w2"][0][i * 256:(i + 1) * 256].reshape(2, P, D_MODEL).transpose(1, 0, 2).reshape(P, UNIT))
        else:
            for e in range(EXPERTS):
                for c in range(FC + 2):
                    if c < FC:
                        both = np.concatenate([a[w][0, e][:, c * 256:(c + 1) * 256] for w in ("moe_w1", "moe_w3")], 1)
                        both = both.reshape(2, 4, P, 512)
                        for half in range(2):
                            put(both[half].transpose(1, 0, 2).reshape(P, UNIT))
                    if c >= 2:
                        put(a["moe_w2"][0, e][(c - 2) * 256:(c - 1) * 256].reshape(2, P, D_MODEL)
                            .transpose(1, 0, 2).reshape(P, UNIT))
    assert n == N_UNITS

    cols = np.zeros((P, N_COLS), np.float32)
    col = lambda x: x.reshape(-1, P).T
    cols[:, V_C:V_C + 8], cols[:, V_CC:V_CC + 8] = col(a["c"][0]), col(a["c_ctx"])
    wsm = np.zeros((P, 576), np.float32)
    gw2 = np.zeros((DEPTH, 33, T), np.float32)
    aux = np.zeros((DEPTH, 4, 2, 2 * D_MODEL), np.float32)
    for l in range(DEPTH):
        b = V_LAYER + l * V_STRIDE
        cols[:, b + V_GPM:b + V_GPM + 8], cols[:, b + V_GPF:b + V_GPF + 8] = col(a["g_pre_mix"][l]), col(a["g_pre_ffn"][l])
        cols[:, b + V_SUB], cols[:, b + V_ON] = a["diff_subln"][l], a["gla_onorm"][l]
        cols[:, b + V_BMOD:b + V_BMOD + 48] = col(a["b_mod"][l])
        wsm[:, l * 256:(l + 1) * 256] = a["w_in"][l][:, 3072:].reshape(KT, P, 32).transpose(1, 0, 2).reshape(P, 256)
        for d in range(2):
            gw2[l, d * RANK:(d + 1) * RANK, d * 256:(d + 1) * 256] = a["gla_gate_w2"][l, d]
        gw2[l, 32] = a["gla_gate_b"][l].reshape(-1)
        for i, (at, g) in enumerate(((2, "g_post_mix"), (5, "g_post_ffn"))):
            aux[l, 0, 0, i * D_MODEL:(i + 1) * D_MODEL] = a["b_mod"][l][at * D_MODEL:(at + 1) * D_MODEL]
            aux[l, 2, 0, i * D_MODEL:(i + 1) * D_MODEL] = a["b_mod"][l][at * D_MODEL:(at + 1) * D_MODEL]
            aux[l, :, 1, i * D_MODEL:(i + 1) * D_MODEL] = a[g][l]
    wsm[:, 512:] = a["router"][0].reshape(KT, P, EXPERTS).transpose(1, 0, 2).reshape(P, 64)
    return {
        "units": units, "x_in": np.ascontiguousarray(a["x"][0]), "ctx_in": np.ascontiguousarray(a["ctx"][0]),
        "const_in": constants(), "cols_in": cols, "wsm_in": wsm, "gw2_in": gw2,
        "lam_in": np.ascontiguousarray(a["diff_lambda"].reshape(1, -1)), "rope_in": rope_constants(), "aux_in": aux,
    }


def kernel(**inputs):
    import concourse.bacc as bacc
    from concourse.bass_utils import run_bass_kernel_spmd as run

    arrays = pack(inputs)
    nc = bacc.Bacc("TRN2", target_bir_lowering=False, num_devices=1)
    args = {k: nc.dram_tensor(k, x.shape, F32, kind="ExternalInput").ap() for k, x in arrays.items()}
    out = nc.dram_tensor("out", (1, LAT, D_MODEL), F32, kind="ExternalOutput").ap()
    with ExitStack() as ctx:
        build(nc, ctx, *(args[k] for k in ("units", "x_in", "ctx_in", "const_in", "cols_in", "wsm_in", "gw2_in",
                                           "lam_in", "rope_in", "aux_in")), out)
    return run(nc, [arrays], core_ids=[0]).results[0]["out"]
```

```python
from contextlib import ExitStack

import concourse.bass as bass
from concourse import mybir

F32 = mybir.dt.float32
F32R = mybir.dt.float32r
I32 = mybir.dt.int32
ACT = mybir.ActivationFunctionType
ALU = mybir.AluOpType
X_AXIS = mybir.AxisListType.X

P = 128
D_MODEL, CTX, LAT, DEPTH = 1024, 256, 256, 2
T = CTX + LAT
TILES = T // P
KT = D_MODEL // P
HEADS, QK, VD = 4, 64, 128
WIDTH = HEADS * VD
RANK = 16
CHUNK = 64
D_FF = 2816
FT = D_FF // P
EXPERTS = 8
N_MOD = 6
GRID_W = 64
ROPE_THETA = 10000.0
EPS = 1e-6
LAM_INIT = (0.2, 0.35550906759096937)

UNIT = 2048
RING = 3
MOD_A = 2 * D_MODEL // 256
MOD_UNITS = N_MOD * D_MODEL // 256
IN_F, IN_K = 6, 6
OUT_UNITS = D_MODEL // 256
UP_UNITS, DOWN_UNITS = FT, FT // 2
FC = D_FF // 256
EXPERT_UNITS = 3 * FC


STAGES = (("mod_a", 0), ("in", 0), ("mod_b", 0), ("mod_a", 1), ("out", 0), ("up", 0), ("down", 0),
          ("in", 1), ("mod_b", 1), ("out", 1), ("moe", 1))
STAGE_UNITS = {"mod_a": MOD_A, "in": IN_F + IN_K, "mod_b": MOD_UNITS - MOD_A, "out": OUT_UNITS,
               "up": UP_UNITS, "down": DOWN_UNITS, "moe": EXPERTS * EXPERT_UNITS}


def unit_numbers():
    at, n = {}, 0
    for stage in STAGES:
        at[stage] = n
        n += STAGE_UNITS[stage[0]]
    return at, n


U, N_UNITS = unit_numbers()

C_IDENT, C_TRI, C_UPPER, C_ONES, C_PERM, C_IOTA = 0, 128, 384, 512, 640, 768
C_SELC, C_EPS, C_DESC, N_CONST = 1024, 1026, 1027, 1040
V_C, V_CC = 0, 8
V_LAYER, V_STRIDE = 16, 82
V_GPM, V_GPF, V_SUB, V_ON, V_BMOD, V_POST = 0, 8, 16, 17, 18, 66
N_COLS = V_LAYER + DEPTH * V_STRIDE + 4


def token_tiles(l, stage):
    return range(TILES) if l == 0 or stage == "mix" else range(CTX // P, TILES)


def mod_unit(l, j):
    return U["mod_a", l] + j if j < MOD_A else U["mod_b", l] + j - MOD_A


def mod_steps(units):
    steps = [[("mod",) + u] + ([("modx",) + units[n - 1]] if n else []) for n, u in enumerate(units)]
    return steps + [[("modx",) + units[-1]]]


def beside(l, stage):
    if (l, stage) == (1, "gla"):
        return {}
    units, step = {(0, "att"): ([(0, j) for j in range(MOD_A, MOD_UNITS)], 2),
                   (1, "att"): ([(1, j) for j in range(MOD_A, MOD_UNITS)], 1),
                   (0, "gla"): ([(1, j) for j in range(MOD_A)], 2)}[l, stage]
    return {n * step: here for n, here in enumerate(mod_steps(units))}


def sides(l):
    return (0, 1) if l == 0 else (1,)


LAST_OF, MID_OF = (CHUNK - 1, 0), (CHUNK // 2 - 1, CHUNK // 2)


def chunk_order(d):
    n = CTX // CHUNK
    return list(range(2 * n)) if d == 0 else list(range(n))[::-1] + list(range(n, 2 * n))[::-1]


def expert_steps():
    steps, m = [], 0
    for c in range(FC + 2):
        here = {}
        if c < FC:
            here["up"] = (m, m + 1)
            m += 2
        if c >= 2:
            here["down"] = m
            m += 1
        steps.append(here)
    assert m == EXPERT_UNITS
    return steps


STEPS = expert_steps()


Z_AFTER, G_AFTER = 0, 2


def attn_items(l):
    return [(h, t) for t in token_tiles(l, "out") for h in range(HEADS)]


def gla_items(l):
    return [(h, t) for t in token_tiles(l, "out") for h in range(HEADS)]


def psum_jobs():
    out = []
    for l in range(DEPTH):
        if l == 0:
            out += [key for here in mod_steps([(0, j) for j in range(MOD_A)]) for key in here]
        out += [("T", l, "mix", k) for k in range(KT)]
        out += [("F", l, f) for f in range(2 * IN_F)]
        out += [("rope", l, b) for b in range(4)]
        out += [("glr", l)]
        for u in range(IN_K):
            out += [("K", l, u, g) for g in range(2)]
            out += [("Z", l, t) for t in range(TILES)] if u == Z_AFTER else []
            out += [("G", l, dp) for dp in range(4)] if u == G_AFTER else []
        n = len(attn_items(l))
        for i in range(n + 2):
            if i < n:
                out += [("S", l, i, 0), ("S", l, i, 1)]
            out += beside(l, "att").get(2 * i, [])
            if 1 <= i <= n:
                out.append(("PT", l, i - 1))
            if i >= 2:
                out.append(("O", l, i - 2))
            out += beside(l, "att").get(2 * i + 1, [])
        out += [("KT", l, dp) for dp in range(4)]
        for dp in range(4):
            out += [("DS", l, dp, 0), ("DS", l, dp, 1)]
        m = len(gla_items(l))
        for i in range(m + 1):
            if i < m:
                out.append(("M", l, i))
            out += beside(l, "gla").get(2 * i, [])
            if i >= 1:
                out.append(("OG", l, i - 1))
        out += [("GB", l, 0, s, h) for s in sides(l) for h in range(2)]
        out += [("MT", l, f) for f in range(KT)]
        out += [("Y", l, u, g) for u in range(OUT_UNITS) for g in range(2 if l == 0 else 1)]
        out += [("GB", l, 1, s, h) for s in sides(l) for h in range(2)]
        out += [("T", l, "ffn", k) for k in range(KT)]
        if l == 0:
            for j in range(UP_UNITS):
                out += [("GU", l, j, 0), ("GU", l, j, 1)]
            out += [("D", l, t, h) for t in range(TILES) for h in range(2)]
        else:
            out += [("H2", q) for q in range(4)] + [("LG",), ("POS",)]
    return {key: n for n, key in enumerate(out)}


JOBS = psum_jobs()
BANKS = 8

BASE = 16512
A_RAW, A_HI, A_LO = 0, 6144, 12288
A_X = 18432
A_ACTT = 22528
A_GATE = 30720
A_V, A_GV, A_GG, A_GQ, A_GK = 34816, 36864, 38912, 40960, 41984
A_GL, A_GT, A_OD, A_GLRT = 43008, 45056, 47104, 49152
A_CONST = 49664
A_COLS = A_CONST + N_CONST
A_WSM = A_COLS + N_COLS
A_GW2 = A_WSM + 576
A_AM = A_GW2 + 512
A_STAT = A_AM + 512
A_ROUTE = A_OD + 1024
A_AT, A_ATS, A_SIL = A_V, 46080, 48128


def release_points():
    at = {}
    for l in range(DEPTH):
        for j in range(MOD_UNITS):
            at[mod_unit(l, j)] = ("job", JOBS["mod", l, j])
        for u in range(IN_F):
            at[U["in", l] + u] = ("job", JOBS["F", l, 2 * u + 1])
        for u in range(IN_K):
            at[U["in", l] + IN_F + u] = ("job", JOBS["K", l, u, 1])
        for u in range(OUT_UNITS):
            at[U["out", l] + u] = ("job", JOBS["Y", l, u, 1 if l == 0 else 0])
    for j in range(UP_UNITS):
        at[U["up", 0] + j] = ("job", JOBS["GU", 0, j, 1])
    for i in range(DOWN_UNITS):
        at[U["down", 0] + i] = ("tile", 2 * i + 1) if i < DOWN_UNITS - 1 else ("job", JOBS["D", 0, TILES - 1, 1])
    return at


RELEASE = release_points()
PASSES = ((0, 0), (0, 1), (1, 0))
HALVES = (slice(0, UNIT // 2), slice(UNIT // 2, UNIT))


def n_keys(t):
    return CTX if t < CTX // P else T


TURN_BANK = 3


def scatter_bank(n, tau):
    return 2 + n if n < 2 or tau == 0 else 4 + n


def up_bank(c, tau):
    return c % 2 if tau == 0 else 2


def build(nc, ctx, units, x_in, ctx_in, const_in, cols_in, wsm_in, gw2_in, lam_in, rope_in, out):
    def at(name, offset, shape, dt=F32):
        size = 1
        for s in shape[1:]:
            size *= s
        return nc.alloc_sbuf_tensor_at(name, shape, dt, offset=BASE + 4 * offset)

    stat_at = [A_STAT]

    def stat(name, n, dt=F32):
        here = stat_at[0]
        stat_at[0] += -(-n // 8) * 8
        return at(name, here, [P, n], dt)

    raw = at("raw", A_RAW, [P, RING, UNIT])
    w_hi = at("w_hi", A_HI, [P, RING, UNIT], F32R)
    w_lo = at("w_lo", A_LO, [P, RING, UNIT], F32R)
    X = at("X", A_X, [P, TILES, D_MODEL])
    act_hi = at("act_hi", A_ACTT, [P, KT, T], F32R)
    act_lo = at("act_lo", A_ACTT + 4096, [P, KT, T], F32R)
    gexp = at("gexp", A_ACTT, [P, 4, 4, T])
    y_ffn = at("y_ffn", A_ACTT, [P, TILES, D_MODEL])
    gate = at("gate", A_GATE, [P, 2, 2, D_MODEL])
    qT = at("qT", A_GATE, [P, HEADS, T])
    kT = at("kT", A_GATE + 2048, [P, HEADS, T])
    states = at("states", A_GATE, [P, 4, 8, VD])
    v = at("v", A_V, [P, TILES, WIDTH])
    og = at("og", A_V, [P, TILES, WIDTH])
    gv = at("gv", A_GV, [P, TILES, WIDTH])
    gg = at("gg", A_GG, [P, TILES, WIDTH])
    y_mix = at("y_mix", A_GV, [P, TILES, D_MODEL])
    xn = at("xn", A_V, [P, TILES, D_MODEL])
    gqT = at("gqT", A_GQ, [P, 2, T])
    gkT = at("gkT", A_GK, [P, 2, T])
    gl = at("gl", A_GL, [P, TILES, T])
    zabs = at("zabs", A_GT, [P, TILES, T])
    GT = at("GT", A_GT, [P, 4, T])
    klT = at("klT", A_GL, [P, 4, TILES, P])
    gla_junk = at("gla_junk", A_GT, [P, P])
    probs = at("probs", A_GL, [P, 2, 2, T])
    probsT = at("probsT", A_GL + 2048, [P, 2, T])
    att_junk = at("att_junk", A_GL + 3072, [P, P])
    rope = at("rope", A_GL + 3584, [P, 2, LAT])
    hf = at("hf", A_GL, [P, RING, T])
    y_junk = at("y_junk", A_GL, [P, D_MODEL])
    glr_hi = at("glr_hi", A_GL + 1536, [P, KT, 32], F32R)
    glr_lo = at("glr_lo", A_GL + 1792, [P, KT, 32], F32R)
    rope_tmp = at("rope_tmp", A_GL + 2176, [P, 2, LAT])
    lam_in_sb = at("lam_in_sb", A_GL, [P, DEPTH, 2, 2, QK])
    lam_prod = at("lam_prod", A_GL + 512, [P, DEPTH, 2, QK])
    od = at("od", A_OD, [P, TILES, WIDTH])
    glrT = at("glrT", A_GLRT, [33, T])
    const = at("const", A_CONST, [P, N_CONST])
    cols = at("cols", A_COLS, [P, N_COLS])
    wsm = at("wsm", A_WSM, [P, 576])
    gw2 = at("gw2", A_GW2, [33, T])
    Am = at("Am", A_AM, [P, 2, 2, P])
    ffnT = at("ffnT", A_AT, [P, FT, T])
    ffn_hi = at("ffn_hi", A_ATS, [P, 2, T], F32R)
    ffn_lo = at("ffn_lo", A_ATS + 1024, [P, 2, T], F32R)
    ffn_sil = at("ffn_sil", A_SIL, [P, 2, T])

    xt_hi = at("xt_hi", A_ACTT, [P, KT, 2, P], F32R)
    xt_lo = at("xt_lo", A_ACTT + 2048, [P, KT, 2, P], F32R)
    h2_hi = at("h2_hi", A_ACTT + 4096, [P, 2, D_MODEL], F32R)
    h2_lo = at("h2_lo", A_ACTT + 6144, [P, 2, D_MODEL], F32R)
    h2T = at("h2T", A_GG, [P, KT, LAT])
    y_moe = at("y_moe", A_GQ, [P, 2, D_MODEL])
    e_sil = at("e_sil", A_GL, [P, 2, 256])
    e_act = at("e_act", A_V, [P, 2, 2, 256])
    e_rows = at("e_rows", A_V + 1024, [P, D_MODEL])
    sel = at("sel", A_GL + 1024, [P, 2, 2 * P], F32R)
    selT = at("selT", A_GL + 512, [P, 2, 2, P], F32R)
    eT_hi = at("eT_hi", A_GL + 1792, [P, 2, 2, 256], F32R)
    eT_lo = at("eT_lo", A_GL + 2816, [P, 2, 2, 256], F32R)
    route = at("route", A_GL + 3840, [P, 2, 6, EXPERTS + 1])
    ey_hi = at("ey_hi", A_OD, [P, D_MODEL], F32R)
    ey_lo = at("ey_lo", A_OD + 1024, [P, D_MODEL], F32R)

    c_act = stat("c_act", 16)
    ssq, std, rstd = stat("ssq", 4), stat("std", 4), stat("rstd", 4)
    modc = at("modc", stat_at[0], [P, DEPTH, N_MOD, KT, 2])
    stat_at[0] += DEPTH * N_MOD * KT * 2
    c_cols = at("c_cols", stat_at[0], [P, KT, 4], F32R)
    stat_at[0] += 4 * KT
    mod_row = at("mod_row", stat_at[0], [4, 256])
    stat_at[0] += 256
    od_ssq, od_std, od_rstd = stat("od_ssq", 16), stat("od_std", 16), stat("od_rstd", 16)
    og_ssq, og_std, og_rstd = stat("og_ssq", 16), stat("og_std", 16), stat("og_rstd", 16)
    sub_gain = stat("sub_gain", DEPTH)
    row_max, neg_max, row_sum, row_inv = (at(n, stat_at[0] + 8 * i, [P, 2, 2]) for i, n in
                                          enumerate(("row_max", "neg_max", "row_sum", "row_inv")))
    stat_at[0] += 32
    neg_lam, lam_sum, lam_exp = stat("neg_lam", 2), stat("lam_sum", 4), stat("lam_exp", 4)
    decay = at("decay", stat_at[0], [P, 4, 8])
    stat_at[0] += 32
    e_cols = at("e_cols", A_GL + 3952, [P, 4])
    e_weight = at("e_weight", A_GL + 3960, [P, 2])
    counts_i = at("counts_i", A_GL + 3968, [P, EXPERTS + 1], I32)
    rt = at("rt", A_GL + 3984, [P, 12])

    psum = nc.alloc_psum_tensor("psum", [P, BANKS, 512], F32)

    ident, ones = const[:, C_IDENT:C_IDENT + P], const[:, C_ONES:C_ONES + P]
    tri = const[:, C_TRI:C_TRI + 2 * P]
    eps = const[:, C_EPS:C_EPS + 1]

    sems = {}

    def sem(name):
        if name not in sems:
            sems[name] = nc.alloc_semaphore(name)
        return sems[name]

    loaded, cols_loaded, const_loaded, rope_loaded, gw2_loaded, stored = (
        sem(n) for n in ("loaded", "cols_loaded", "const_loaded", "rope_loaded", "gw2_loaded", "stored"))
    x_loaded = [sem("ctx_loaded"), sem("x_loaded")]
    arrived = [sem(f"arrived{s}") for s in range(RING)]
    hi_ready, lo_ready, units_used = sem("hi_ready"), sem("lo_ready"), sem("units_used")
    filled = sem("filled")
    emptied = [sem(f"emptied{b}") for b in range(BANKS)]

    def bank(key):
        return psum[:, JOBS[key] % BANKS, :]

    def wait_filled(eng, key):
        eng.wait_ge(filled, JOBS[key] + 1)

    def wait_copied(eng, key):
        eng.wait_ge(emptied[JOBS[key] % BANKS], JOBS[key] // BANKS + 1)

    def wait_emptied(pe, key):
        if JOBS[key] >= BANKS:
            pe.wait_ge(emptied[JOBS[key] % BANKS], JOBS[key] // BANKS)

    def wait_released(eng, n):
        kind, count = RELEASE[n]
        eng.wait_ge(filled if kind == "job" else sem("down_tiles"), count + 1)

    def x_added(stage, l, t):
        return sem(f"x_{stage}{l}_{t}")

    def esem(name, tau):
        return sem(f"e_{name}{tau}")

    def wait_expert_unit_used(eng, e, m):
        before = m < 0
        m %= EXPERT_UNITS
        for c, here in enumerate(STEPS):
            for name, unit, chunk in (("half", here.get("up", (-1,))[0], c), ("up", here.get("up", (-1,))[-1], c),
                                      ("down", here.get("down", -1), c - 2)):
                if unit == m:
                    for tau in range(2):
                        eng.wait_ge(esem(name, tau), (e + (0 if before else 1)) * FC + (chunk + 1))

    def both(eng, many, work, signals):
        work(0)
        with eng.If(many):
            work(1)
            eng.nop()
        with eng.Else():
            for name, count in signals:
                eng.sem_inc(esem(name, 1), count)

    assert BASE + 4 * stat_at[0] <= nc.sbuf_usable_end, stat_at[0]
    weights, acts = (w_hi, w_lo), (act_hi, act_lo)
    y_mix_of, y_ffn_of, y_moe_of = (lambda t: y_mix[:, t, :]), (lambda t: y_ffn[:, t, :]), (lambda t: y_moe[:, t - 2, :])

    block = ctx.enter_context(nc.Block())

    @block.sync
    def _(sp):
        def load(slot, n):
            sp.dma_start(raw[:, slot, :], units[bass.ds(n, 1)].rearrange("a p n -> (a p) n")).then_inc(arrived[slot], 16)

        for n in range(RING):
            load(n, n)
        rounds = N_UNITS // RING
        with sp.Fori(1, rounds) as i:
            for s in range(RING):
                sp.wait_ge(lo_ready, i * RING + (s - RING + 1))
                load(s, i * RING + s)
        for n in range(rounds * RING, N_UNITS + RING):
            sp.wait_ge(lo_ready, n - RING + 1)
            load(n % RING, min(n, N_UNITS - 1))
        for t in token_tiles(1, "out"):
            sp.wait_ge(x_added("ffn", 1, t), 1)
        sp.dma_start(out[0].rearrange("(t p) d -> p t d", p=P), X[:, CTX // P:TILES, :]).then_inc(stored, 16)
        sp.wait_ge(stored, 16)

    @block.gpsimd
    def _(pool):
        def add(l, stage, y):
            for n, t in enumerate(token_tiles(l, "out")):
                if t % 2 == 0:
                    pool.wait_ge(sem(f"y_{stage}{l}"), n + 1)
                    pool.tensor_tensor(X[:, t, :], X[:, t, :], y(t), ALU.add).then_inc(x_added(stage, l, t), 1)

        pool.memset(Am[:, :, :, :], 0.0).then_inc(sem("zeros"), 1)
        pool.wait_ge(sem("zeros"), 1)
        pool.memset(glrT[32:33, :], 1.0).then_inc(sem("zeros"), 1)
        pool.wait_ge(sem("zeros"), 2)
        for l in range(DEPTH):
            if l == 1:
                pool.wait_ge(filled, JOBS["T", 1, "mix", 0] + 1)
            pool.dma_start(rope[:, :, :], rope_in).then_inc(rope_loaded, 16)
            if l == 1:
                pool.wait_ge(filled, JOBS["Z", 0, TILES - 1] + 1)
            pool.dma_start(gw2[:, :], gw2_in[l]).then_inc(gw2_loaded, 16)
            add(l, "mix", y_mix_of)
            if l == 0:
                add(0, "ffn", y_ffn_of)
        add(1, "ffn", y_moe_of)

    @block.scalar
    def _(act):
        split = [0]

        def split_upto(n):
            while split[0] <= min(n, U["moe", 1] - 1):
                i = split[0]
                act.wait_ge(arrived[i % RING], 16 * (i // RING + 1))
                if i >= RING:
                    wait_released(act, i - RING)
                for part in HALVES:
                    act.activation(w_hi[:, i % RING, part], raw[:, i % RING, part], ACT.Copy).then_inc(hi_ready, 1)
                split[0] += 1

        def copy_out(key, dst, src, scale=1.0):
            wait_filled(act, key)
            act.activation(dst, src, ACT.Copy, scale=scale).then_inc(emptied[JOBS[key] % BANKS], 1)

        act.dma_start(cols[:, :], cols_in).then_inc(cols_loaded, 16)
        act.dma_start(const[:, :], const_in).then_inc(const_loaded, 16)
        for i, src in enumerate((ctx_in, x_in)):
            act.dma_start(X[:, 2 * i:2 * i + 2, :],
                          src.rearrange("(t p) d -> p t d", p=P)).then_inc(x_loaded[i], 16)
        act.dma_start(wsm[:, :], wsm_in).then_inc(loaded, 16)
        act.dma_start(lam_in_sb[:, :, :, :, :].rearrange("p a b c d -> p (a b c d)"),
                      lam_in.to_broadcast([P, DEPTH * 4 * QK])).then_inc(loaded, 16)
        act.wait_ge(cols_loaded, 16)
        act.activation(c_act[:, :], cols[:, 0:16], ACT.Silu).then_inc(sem("c_act"), 1)
        act.wait_ge(sem("c_act"), 1)
        for i in range(2):
            act.activation(c_cols[:, :, 2 * i], c_act[:, 8 * i:8 * i + 8], ACT.Copy).then_inc(sem("c_hi"), 1)

        def mod_step(kind, l, j):
            if kind == "mod":
                split_upto(mod_unit(l, j) + 2)
                if (l, j) != (0, 0):
                    wait_filled(act, ("modx", l, j - 1) if j else ("modx", l - 1, MOD_UNITS - 1))
                copy_out(("mod", l, j), mod_row[:, :], bank(("mod", l, j))[0:4, 0:256])

        def beside_item(l, stage, place):
            for key in beside(l, stage).get(place, ()):
                mod_step(*key)

        def gates_on_all(l, w):
            for s in sides(l):
                for h in range(2):
                    key = ("GB", l, w, s, h)
                    copy_out(key, gate[:, w, s, h * 512:(h + 1) * 512], bank(key))

        def mean_square(name, l, stage, tiles, src, junk, wait, some=None):
            done = sem(f"{name}_{stage}{l}")
            for n, t in enumerate(tiles):
                if some is not None and n not in some:
                    continue
                wait(n)
                act.activation(junk(t), src(t), ACT.Square, accum_out=ssq[:, t:t + 1]).then_inc(done, 1)
                act.wait_ge(done, 2 * n + 1)
                act.activation(std[:, t:t + 1], ssq[:, t:t + 1], ACT.Sqrt, bias=eps, scale=1.0 / D_MODEL).then_inc(done, 1)

        def norm(l, stage, some=None):
            tiles = token_tiles(l, stage)
            before = {("mix", 1): ("ffn", 0), ("ffn", 0): ("mix", 0), ("ffn", 1): ("mix", 1)}.get((stage, l))
            mean_square("norm", l, stage, tiles, lambda t: X[:, t, :], lambda t: xn[:, t, :],
                        lambda n: act.wait_ge(x_loaded[n // 2], 16) if before is None else
                        act.wait_ge(x_added(*before, tiles[n]), 1), some)

        def halves(l, stage):
            return (0, 1) if l == 0 or stage == "mix" else (1,)

        def modulated(l, stage):
            w = 0 if stage == "mix" else 1
            act.wait_ge(sem(f"scale{l}"), 4 * (w + 1))
            for k in range(KT):
                key = ("T", l, stage, k)
                wait_filled(act, key)
                sides = halves(l, stage)
                if k >= RING and len(sides) == 2:
                    act.wait_ge(sem(f"act_lo_{stage}{l}"), k - RING + 1)
                for s in sides:
                    dst = h2T[:, k, :] if len(sides) == 1 else hf[:, k % RING, s * 256:(s + 1) * 256]
                    ins = act.activation(dst, bank(key)[:, s * 256:(s + 1) * 256], ACT.Identity,
                                         scale=modc[:, l, 3 * w + 1, k, s:s + 1], bias=modc[:, l, 3 * w, k, s:s + 1])
                ins.then_inc(emptied[JOBS[key] % BANKS], 1)

        def gate_logs(l):
            done = sem(f"gate_log{l}")
            act.wait_ge(sem(f"roped{l}"), 4)
            for t in range(TILES):
                wait_filled(act, ("Z", l, t))
                act.activation(zabs[:, t, :], bank(("Z", l, t)), ACT.Abs).then_inc(sem(f"zabs{l}"), 1)
            for t in range(TILES):
                act.wait_ge(sem(f"zabs{l}"), t + 1)
                act.activation(zabs[:, t, :], zabs[:, t, :], ACT.Exp, scale=-1.0).then_inc(done, 1)
            act.wait_ge(done, TILES)
            for t in range(TILES):
                act.activation(zabs[:, t, :], zabs[:, t, :], ACT.Ln, bias=const[:, C_ONES:C_ONES + 1]).then_inc(done, 1)

        def gate_exps(l, dp):
            done = sem(f"gexp{l}")
            act.wait_ge(sem(f"gsub{l}"), 2 * dp + 2)
            act.activation(gexp[:, 1, dp, :], gexp[:, 0, dp, :], ACT.Exp, scale=-1.0).then_inc(done, 1)
            act.activation(gexp[:, 2, dp, :], gexp[:, 2, dp, :], ACT.Exp).then_inc(done, 1)
            act.wait_ge(done, 4 + 3 * dp + 1)
            act.activation(gexp[:, 0, dp, :], gexp[:, 0, dp, :], ACT.Exp).then_inc(done, 1)

        def in_projection(l):
            act.wait_ge(loaded, 32)
            act.activation(glr_hi[:, :, :], wsm[:, l * 256:(l + 1) * 256].rearrange("p (k n) -> p k n", n=32),
                           ACT.Copy).then_inc(sem(f"glr_hi{l}"), 1)
            for u in range(IN_F):
                split_upto(U["in", l] + u + 2)
                for f in (2 * u, 2 * u + 1):
                    dst = (qT[:, f, :] if f < 4 else kT[:, f - 4, :] if f < 8 else
                           gqT[:, f - 8, :] if f < 10 else gkT[:, f - 10, :])
                    copy_out(("F", l, f), dst, bank(("F", l, f)), QK ** -0.5 if f in (8, 9) else 1.0)
            for u in range(IN_K):
                split_upto(U["in", l] + IN_F + u + 2)
                for g in range(2):
                    dst = (v, gv, gg)[u // 2][:, 2 * g:2 * g + 2, (u % 2) * 256:(u % 2 + 1) * 256]
                    key = ("K", l, u, g)
                    copy_out(key, dst, bank(key).rearrange("p (t n) -> p t n", t=2))
                if u == Z_AFTER:
                    gate_logs(l)
                if u == G_AFTER:
                    for dp in range(4):
                        copy_out(("G", l, dp), GT[:, dp, :], bank(("G", l, dp)))
            wait_filled(act, ("K", l, IN_K - 1, 1))
            for dp in range(4):
                wait_copied(act, ("G", l, dp))
                act.activation(gexp[:, 3, dp, :], GT[:, dp, :], ACT.Exp).then_inc(sem(f"gexp{l}"), 1)

        def attention(l):
            items = attn_items(l)
            n = len(items)
            for i in range(n + 2):
                if i < n:
                    b, keys = i % 2, n_keys(items[i][1])
                    act.wait_ge(sem(f"neg_max{l}"), i + 1)
                    if i >= 2:
                        wait_filled(act, ("PT", l, i - 2))
                    for j in range(2):
                        act.activation(probs[:, b, j, 0:keys], bank(("S", l, i, j))[:, 0:keys], ACT.Exp,
                                       scale=QK ** -0.5, bias=neg_max[:, b, j:j + 1],
                                       accum_out=row_sum[:, b, j:j + 1]).then_inc(
                                           emptied[JOBS["S", l, i, j] % BANKS], 1)
                if i < 4:
                    gate_exps(l, i)
                beside_item(l, "att", 2 * i)
                if i == 1:
                    act.wait_ge(sem(f"gsub{l}"), 8)
                    act.wait_ge(sem(f"gexp{l}"), 4)
                if 1 <= i <= n:
                    key, keys = ("PT", l, i - 1), n_keys(items[i - 1][1])
                    if i >= 3:
                        wait_filled(act, ("O", l, i - 3))
                    copy_out(key, probsT[:, (i - 1) % 2, 0:keys], bank(key)[:, 0:keys])
                if i >= 2:
                    key, (h, t) = ("O", l, i - 2), items[i - 2]
                    wait_filled(act, key)
                    act.activation(od[:, t, h * P:(h + 1) * P], bank(key)[:, 0:P], ACT.Copy)
                    if i >= 3:
                        wait_copied(act, ("O", l, i - 3))
                    act.activation(att_junk[:, :], bank(key)[:, 0:P], ACT.Square,
                                   accum_out=od_ssq[:, 4 * t + h:4 * t + h + 1]).then_inc(
                                       emptied[JOBS[key] % BANKS], 1)
                beside_item(l, "att", 2 * i + 1)

        def head_std(l, dst, src, last):
            t0 = 4 * token_tiles(l, "out")[0]
            wait_copied(act, last)
            act.activation(dst[:, t0:16], src[:, t0:16], ACT.Sqrt, bias=eps, scale=1.0 / VD).then_inc(sem(f"head_std{l}"), 1)

        def gla(l):
            for dp in range(4):
                copy_out(("KT", l, dp), klT[:, dp, :, :].rearrange("p t n -> p (t n)"), bank(("KT", l, dp)))
            t0 = token_tiles(l, "out")[0]
            act.activation(gg[:, t0:TILES, :], gg[:, t0:TILES, :], ACT.Silu).then_inc(sem(f"gg_silu{l}"), 1)
            for i, (h, t) in enumerate(gla_items(l)):
                beside_item(l, "gla", 2 * i)
                key = ("OG", l, i)
                wait_filled(act, key)
                act.activation(og[:, t, h * P:(h + 1) * P], bank(key)[:, 0:P], ACT.Copy)
                if i >= 1:
                    wait_copied(act, ("OG", l, i - 1))
                act.activation(gla_junk[:, :], bank(key)[:, 0:P], ACT.Square,
                               accum_out=og_ssq[:, 4 * t + h:4 * t + h + 1]).then_inc(emptied[JOBS[key] % BANKS], 1)
            head_std(l, og_std, og_ssq, ("OG", l, len(gla_items(l)) - 1))

        def merged(l):
            act.wait_ge(sem("lam_ready"), 1)
            lo = token_tiles(l, "out")[0] * P
            for f in range(KT):
                key = ("MT", l, f)
                wait_filled(act, key)
                if f >= RING:
                    act.wait_ge(sem(f"act_lo_out{l}"), f - RING + 1)
                gain = sub_gain[:, l:l + 1] if f < 4 else cols[:, V_LAYER + l * V_STRIDE + V_ON:][:, 0:1]
                act.activation(hf[:, f % RING, lo:T], bank(key)[:, lo:T], ACT.Copy, scale=gain).then_inc(
                    emptied[JOBS[key] % BANKS], 1)

        def out_projection(l):
            for u in range(OUT_UNITS):
                split_upto(U["out", l] + u + 2)
                for g in range(2 if l == 0 else 1):
                    key, t = ("Y", l, u, g), 2 * g if l == 0 else 2
                    copy_out(key, y_mix[:, t:t + 2, u * 256:(u + 1) * 256], bank(key).rearrange("p (t n) -> p t n", t=2))
            act.wait_ge(sem(f"act_lo_out{l}"), KT)
            mean_square("post", l, "mix", token_tiles(l, "out"), y_mix_of, lambda t: y_junk[:, :],
                        lambda n: wait_copied(act, key))
            gates_on_all(l, 1)

        def dense_ffn():
            for j in range(UP_UNITS):
                split_upto(U["up", 0] + j + 2)
                key = ("GU", 0, j, 0)
                wait_filled(act, key)
                if j >= 2:
                    wait_copied(act, ("GU", 0, j - 2, 1))
                act.activation(ffn_sil[:, j % 2, :], bank(key), ACT.Silu).then_inc(emptied[JOBS[key] % BANKS], 1)
            for f in range(FT):
                split_upto(U["down", 0] + (f + 1) // 2 + 1)
                if f == 0:
                    wait_copied(act, ("GU", 0, FT - 1, 1))
                if f >= 2:
                    act.wait_ge(sem("down_tiles"), f - 1)
                act.activation(ffn_hi[:, f % 2, :], ffnT[:, f, :], ACT.Copy).then_inc(sem("ffn_hi"), 1)
            for t in range(TILES):
                for h in range(2):
                    key = ("D", 0, t, h)
                    copy_out(key, y_ffn[:, t, h * 512:(h + 1) * 512], bank(key))

                def copied(n):
                    for h in range(2):
                        wait_copied(act, ("D", 0, n, h))

                mean_square("post", 0, "ffn", range(TILES), y_ffn_of, lambda t: y_junk[:, :], copied, (t,))

        for l in range(DEPTH):
            if l == 0:
                for n, here in enumerate(mod_steps([(0, j) for j in range(MOD_A)])):
                    for key in here:
                        mod_step(*key)
                    if n == 2:
                        act.wait_ge(const_loaded, 16)
                    if 2 <= n < 2 + TILES:
                        norm(0, "mix", (n - 2,))
                act.wait_ge(sem("lam_sum"), 1)
                act.activation(lam_exp[:, :], lam_sum[:, :], ACT.Exp).then_inc(sem("lam_exp"), 1)
            else:
                norm(l, "mix")
            modulated(l, "mix")
            in_projection(l)
            attention(l)
            head_std(l, od_std, od_ssq, ("O", l, len(attn_items(l)) - 1))
            gla(l)
            gates_on_all(l, 0)
            merged(l)
            out_projection(l)
            norm(l, "ffn")
            modulated(l, "ffn")
            if l == 0:
                dense_ffn()

        for q in range(4):
            key = ("H2", q)
            wait_filled(act, key)
            act.activation(h2_hi[:, q // 2, (q % 2) * 512:(q % 2 + 1) * 512], bank(key), ACT.Copy).then_inc(sem("h2_hi"), 1)
        act.wait_ge(sem("top_gap"), 1)
        act.activation(rt[:, 4:6], rt[:, 4:6], ACT.Exp).then_inc(sem("top_exp"), 1)
        wait_copied(act, ("POS",))

        def split_expert(e, start, stop):
            for m in range(start, stop):
                n = U["moe", 1] + m
                act.wait_ge(arrived[n % RING], e * (16 * EXPERT_UNITS // RING) + 16 * (n // RING + 1))
                wait_expert_unit_used(act, e, m - RING)
                for part in HALVES:
                    act.activation(w_hi[:, n % RING, part], raw[:, n % RING, part], ACT.Copy).then_inc(hi_ready, 1)

        def copy_rows(e, tau):
            if tau:
                act.wait_ge(esem("columns", 0), e * 2 + 2)
            for b in range(2):
                act.wait_ge(esem("rows", tau), e * 2 + (b + 1))
                act.activation(e_rows[:, b * 512:(b + 1) * 512], psum[:, b, :], ACT.Copy).then_inc(esem("rows_copy", tau), 1)

        def columns_high(e, tau):
            for b in range(2):
                act.wait_ge(esem("columns", tau), e * 2 + (b + 1))
                act.activation(xt_hi[:, 4 * b:4 * b + 4, tau, :], psum[:, b, :].rearrange("p (k n) -> p k n", n=P),
                               ACT.Copy).then_inc(esem("xt_hi", tau), 1)

        def gathered_second(e, many):
            with act.If(many):
                copy_rows(e, 1)
                columns_high(e, 1)
                act.nop()
            with act.Else():
                act.sem_inc(esem("rows_copy", 1), 2)
                act.sem_inc(esem("xt_hi", 1), 2)

        split_expert(0, 0, RING)
        many = act.value_load(counts_i[0:1, 0:1], min_val=0, max_val=LAT) > P
        copy_rows(0, 0)
        columns_high(0, 0)
        gathered_second(0, many)
        with act.Fori(0, EXPERTS) as e:
            many = act.value_load(counts_i[0:1, bass.ds(e, 1)], min_val=0, max_val=LAT) > P
            many_next = act.value_load(counts_i[0:1, bass.ds(e + 1, 1)], min_val=0, max_val=LAT) > P

            def silu(c, tau):
                act.wait_ge(esem("up", tau), (e + 1) * FC + (c + 1))
                if c:
                    act.wait_ge(esem("act", tau), e * FC + (c + 1))
                act.activation(e_sil[:, tau, :], psum[:, up_bank(c, tau), 0:256], ACT.Silu).then_inc(esem("sil", tau), 1)

            def copy_selT(tau):
                act.wait_ge(esem("selT", tau), e + 1)
                act.activation(selT[:, tau, :, :], psum[:, TURN_BANK, 0:256].rearrange("p (t n) -> p t n", t=2),
                               ACT.Copy).then_inc(esem("selT_copy", tau), 1)

            def turned(c, tau):
                act.wait_ge(esem("turn", tau), e * FC + (c + 1))
                if c >= 2:
                    act.wait_ge(esem("down", tau), (e + 1) * FC + (c - 1))
                act.activation(eT_hi[:, tau, c % 2, :], psum[:, TURN_BANK, 0:256], ACT.Copy).then_inc(esem("eT_hi", tau), 1)

            def output(tau):
                act.wait_ge(esem("down", tau), (e + 2) * FC)
                if tau:
                    act.wait_ge(esem("scatter", 0), (e + 1) * 4)
                for h in range(2):
                    act.activation(ey_hi[:, h * 512:(h + 1) * 512], psum[:, 4 + 2 * tau + h, :], ACT.Copy).then_inc(
                        esem("ey_hi", tau), 1)

            done = RING
            for c in range(FC):
                split_expert(e, done, STEPS[c]["up"][1] + RING)
                done = STEPS[c]["up"][1] + RING
                both(act, many, lambda tau: silu(c, tau), [("sil", 1)])
                if c == 0:
                    both(act, many, copy_selT, [("selT_copy", 1)])
                else:
                    both(act, many, lambda tau: turned(c - 1, tau), [("eT_hi", 1)])
            split_expert(e, done, EXPERT_UNITS + 1)
            both(act, many, lambda tau: turned(FC - 1, tau), [("eT_hi", 1)])
            split_expert(e, EXPERT_UNITS + 1, EXPERT_UNITS + 2)
            copy_rows(e + 1, 0)
            output(0)
            columns_high(e + 1, 0)
            gathered_second(e + 1, many_next)
            with act.If(many):
                output(1)
                act.nop()
            with act.Else():
                act.sem_inc(esem("ey_hi", 1), 2)
            split_expert(e, EXPERT_UNITS + 2, EXPERT_UNITS + 3)
        for tau in range(2):
            act.wait_ge(esem("added", tau), EXPERTS * 4 + 1)
        mean_square("post", 1, "ffn", (2, 3), y_moe_of, lambda t: y_junk[:, :], lambda n: None)

    @block.vector
    def _(dve):
        steps = [0]

        def link(ins):
            steps[0] += 1
            ins.then_inc(sem("dve_step"), 1)
            dve.wait_ge(sem("dve_step"), steps[0])

        split = [0]

        def split_upto(n):
            while split[0] <= min(n, U["moe", 1] - 1):
                i = split[0]
                for half, part in enumerate(HALVES):
                    dve.wait_ge(hi_ready, 2 * i + half + 1)
                    ins = dve.tensor_tensor(w_lo[:, i % RING, part], raw[:, i % RING, part],
                                            w_hi[:, i % RING, part].bitcast(F32), ALU.subtract)
                ins.then_inc(lo_ready, 1)
                split[0] += 1

        def empties(ins, key):
            ins.then_inc(emptied[JOBS[key] % BANKS], 1)

        def lambdas():
            dve.wait_ge(loaded, 32)
            link(dve.tensor_tensor(lam_prod[:, :, :, :], lam_in_sb[:, :, :, 0, :], lam_in_sb[:, :, :, 1, :], ALU.mult))
            dve.tensor_reduce(lam_sum[:, :], lam_prod[:, :, :, :].rearrange("p a b d -> p (a b) d"), X_AXIS,
                              ALU.add).then_inc(sem("lam_sum"), 1)
            dve.wait_ge(sem("lam_exp"), 1)
            for l in range(DEPTH):
                dve.scalar_tensor_tensor(neg_lam[:, l:l + 1], lam_exp[:, 2 * l + 1:2 * l + 2], LAM_INIT[l],
                                         lam_exp[:, 2 * l:2 * l + 1], ALU.subtract, ALU.subtract)
                ins = dve.tensor_scalar(sub_gain[:, l:l + 1], cols[:, V_LAYER + l * V_STRIDE + V_SUB:][:, 0:1],
                                        1.0 - LAM_INIT[l], None, ALU.mult)
            ins.then_inc(sem("lam_ready"), 1)

        dve.wait_ge(sem("c_hi"), 2)
        for i in range(2):
            dve.tensor_tensor(c_cols[:, :, 2 * i + 1], c_act[:, 8 * i:8 * i + 8],
                              c_cols[:, :, 2 * i].bitcast(F32), ALU.subtract).then_inc(sem("c_lo"), 1)

        def mod_step(kind, l, j, ahead=2):
            if kind == "mod":
                split_upto(mod_unit(l, j) + ahead)
                return
            key, base, field, k = ("modx", l, j), V_LAYER + l * V_STRIDE, j // 4, 2 * (j % 4)
            wait_filled(dve, key)
            dst = modc[:, l, field, k:k + 2, :]
            two_sides = lambda at: cols[:, base + at:][:, 0:2].unsqueeze(2).to_broadcast([P, 2, 2])
            empties(dve.tensor_tensor(dst, bank(key)[:, 0:4].rearrange("p (k s) -> p k s", k=2), two_sides(V_BMOD + 2 * j),
                                      ALU.add), key)
            w, part = divmod(field, 3)
            if part:
                wait_copied(dve, key)
            if part == 1:
                dve.scalar_tensor_tensor(dst, dst, 1.0, two_sides((V_GPM, V_GPF)[w] + k), ALU.add,
                                         ALU.mult).then_inc(sem(f"scale{l}"), 1)
            elif part == 2:
                dve.tensor_tensor(dst, dst, two_sides(V_POST + 8 * w + k), ALU.mult).then_inc(sem(f"gate_cols{l}"), 1)

        def beside_item(l, stage, place):
            for key in beside(l, stage).get(place, ()):
                mod_step(*key, ahead=1)

        def norm(l, stage, some=None):
            tiles = token_tiles(l, stage)
            for n, t in enumerate(tiles):
                if some is not None and n not in some:
                    continue
                dve.wait_ge(sem(f"norm_{stage}{l}"), 2 * n + 2)
                link(dve.reciprocal(rstd[:, t:t + 1], std[:, t:t + 1]))
                dve.tensor_scalar(xn[:, t, :], X[:, t, :], rstd[:, t:t + 1], None, ALU.mult).then_inc(
                    sem(f"xn_{stage}{l}"), 1)

        def low_parts(l, stage, lo):
            for k in range(KT):
                wait_copied(dve, ("MT", l, k) if stage == "out" else ("T", l, stage, k))
                dve.tensor_copy(act_hi[:, k, lo:T], hf[:, k % RING, lo:T]).then_inc(sem(f"act_hi_{stage}{l}"), 1)
                dve.wait_ge(sem(f"act_hi_{stage}{l}"), k + 1)
                dve.tensor_tensor(act_lo[:, k, lo:T], hf[:, k % RING, lo:T], act_hi[:, k, lo:T].bitcast(F32),
                                  ALU.subtract).then_inc(sem(f"act_lo_{stage}{l}"), 1)

        def in_projection(l):
            dve.wait_ge(sem(f"glr_hi{l}"), 1)
            dve.tensor_tensor(glr_lo[:, :, :], wsm[:, l * 256:(l + 1) * 256].rearrange("p (k n) -> p k n", n=32),
                              glr_hi[:, :, :].bitcast(F32), ALU.subtract).then_inc(sem(f"glr_lo{l}"), 1)
            split_upto(U["in", l] + IN_F + 1)
            rotate(l)
            key = ("glr", l)
            wait_filled(dve, key)
            empties(dve.tensor_copy(glrT[0:32, :], bank(key)[0:32, :]), key)
            split_upto(U["in", l] + IN_F + 2)
            for t in range(TILES):
                key = ("Z", l, t)
                dve.wait_ge(sem(f"zabs{l}"), t + 1)
                empties(dve.tensor_scalar(gl[:, t, :], bank(key), 0.0, None, ALU.min), key)
            for t in range(TILES):
                wait_copied(dve, ("Z", l, t))
                dve.wait_ge(sem(f"gate_log{l}"), TILES + t + 1)
                dve.tensor_tensor(gl[:, t, :], gl[:, t, :], zabs[:, t, :], ALU.subtract).then_inc(sem(f"gl{l}"), 1)
            split_upto(U["mod_b", l] + 1)
            wait_filled(dve, ("K", l, IN_K - 1, 1))
            for dp in range(4):
                d = dp // 2
                wait_copied(dve, ("G", l, dp))
                g = by_chunk(GT[:, dp, :])
                at_chunk = lambda i: g[:, :, i:i + 1].to_broadcast([P, T // CHUNK, CHUNK])
                dve.tensor_tensor(by_chunk(gexp[:, 0, dp, :]), g, at_chunk(MID_OF[d]), ALU.subtract).then_inc(sem(f"gsub{l}"), 1)
                dve.tensor_tensor(by_chunk(gexp[:, 2, dp, :]), at_chunk(LAST_OF[d]), g, ALU.subtract).then_inc(sem(f"gsub{l}"), 1)

        by_chunk = lambda a: a.rearrange("p (c n) -> p c n", n=CHUNK)

        def gate_products(l, dp):
            d, pair = divmod(dp, 2)
            dve.wait_ge(sem(f"gexp{l}"), 4 + 3 * (dp + 1))
            link(dve.tensor_copy(decay[:, dp, :], by_chunk(gexp[:, 3, dp, :])[:, :, LAST_OF[d]]))
            for kind, other in ((2, gkT), (0, gqT), (1, gkT), (3, gqT)):
                dve.tensor_tensor(gexp[:, kind, dp, :], gexp[:, kind, dp, :], other[:, pair, :],
                                  ALU.mult).then_inc(sem(f"gmul{l}"), 1)

        def rotate(l):
            cos, sin = (rope[:, i:i + 1, :].to_broadcast([P, 2, LAT]) for i in range(2))
            dve.wait_ge(rope_loaded, 16 * (l + 1))
            for b in range(4):
                key = ("rope", l, b)
                dst = (qT if b < 2 else kT)[:, 2 * (b % 2):2 * (b % 2) + 2, CTX:T]
                wait_filled(dve, key)
                empties(dve.tensor_tensor(rope_tmp[:, :, :], bank(key).rearrange("p (h n) -> p h n", h=2), sin,
                                          ALU.mult), key)
                link(dve.tensor_tensor(dst, dst, cos, ALU.mult))
                wait_copied(dve, key)
                dve.tensor_tensor(dst, dst, rope_tmp[:, :, :], ALU.add).then_inc(sem(f"roped{l}"), 1)
                dve.wait_ge(sem(f"roped{l}"), b + 1)

        def attention(l):
            items = attn_items(l)
            n = len(items)
            for i in range(n + 1):
                if i >= 1:
                    b, keys = (i - 1) % 2, n_keys(items[i - 1][1])
                    for j in range(2):
                        wait_copied(dve, ("S", l, i - 1, j))
                    link(dve.reciprocal(row_inv[:, b, :], row_sum[:, b, :]))
                    link(dve.tensor_scalar(row_inv[:, b, 1:2], row_inv[:, b, 1:2], neg_lam[:, l:l + 1], None, ALU.mult))
                    link(dve.tensor_scalar(probs[:, b, 1, 0:keys], probs[:, b, 1, 0:keys], row_inv[:, b, 1:2], None,
                                           ALU.mult))
                    dve.scalar_tensor_tensor(probs[:, b, 0, 0:keys], probs[:, b, 0, 0:keys], row_inv[:, b, 0:1],
                                             probs[:, b, 1, 0:keys], ALU.mult, ALU.add).then_inc(sem(f"probs{l}"), 1)
                if i < n:
                    b, keys = i % 2, n_keys(items[i][1])
                    for j in range(2):
                        wait_filled(dve, ("S", l, i, j))
                        ins = dve.tensor_reduce(row_max[:, b, j:j + 1], bank(("S", l, i, j))[:, 0:keys], X_AXIS, ALU.max)
                    link(ins)
                    dve.tensor_scalar(neg_max[:, b, :], row_max[:, b, :], -QK ** -0.5, None, ALU.mult).then_inc(
                        sem(f"neg_max{l}"), 1)
                if 1 <= i <= 4:
                    gate_products(l, i - 1)
                for place in (2 * i, 2 * i + 1):
                    beside_item(l, "att", place)
            heads_normed(l, od, od_std, od_rstd, 1)

        def heads_normed(l, dst, s, r, count):
            t0 = token_tiles(l, "out")[0]
            dve.wait_ge(sem(f"head_std{l}"), count)
            link(dve.reciprocal(r[:, 4 * t0:16], s[:, 4 * t0:16]))
            part = dst[:, t0:TILES, :].rearrange("p t (h n) -> p (t h) n", n=P)
            dve.tensor_tensor(part, part, r[:, 4 * t0:16].unsqueeze(2).to_broadcast([P, 16 - 4 * t0, P]),
                              ALU.mult).then_inc(sem(f"merged{l}"), 1)

        def gla(l):
            for dp in range(4):
                order = chunk_order(dp // 2)
                for n in range(7):
                    here, after = order[n], order[n + 1]
                    key = ("DS", l, dp, here % 2)
                    ds = bank(key)[:, (here // 2) * P:(here // 2 + 1) * P]
                    if n < 2:
                        wait_filled(dve, key)
                    if n == 0:
                        ins = dve.tensor_copy(states[:, dp, after, :], ds)
                    else:
                        ins = dve.scalar_tensor_tensor(states[:, dp, after, :], states[:, dp, here, :],
                                                       decay[:, dp, here:here + 1], ds, ALU.mult, ALU.add)
                    if n in (5, 6):
                        empties(ins, key)
                        wait_copied(dve, key)
                    else:
                        link(ins)
            for i, (h, t) in enumerate(gla_items(l)):
                if i:
                    beside_item(l, "gla", 2 * i - 2)
                key = ("M", l, i)
                wait_filled(dve, key)
                if i >= 2:
                    wait_filled(dve, ("OG", l, i - 2))
                elif l == 0:
                    dve.wait_ge(sem("zeros"), 2)
                elif i < 2:
                    wait_filled(dve, ("OG", 0, len(gla_items(0)) - 1))
                empties(dve.copy_predicated(Am[:, i % 2, :, :].rearrange("p d n -> p (d n)"), tri.bitcast(I32),
                                            bank(key)[:, 0:2 * P]), key)
            t0 = token_tiles(l, "out")[0]
            dve.wait_ge(sem(f"gg_silu{l}"), 1)
            wait_copied(dve, ("OG", l, len(gla_items(l)) - 1))
            link(dve.tensor_tensor(og[:, t0:TILES, :], og[:, t0:TILES, :], gg[:, t0:TILES, :], ALU.mult))
            heads_normed(l, og, og_std, og_rstd, 2)

        def residual(l, stage, y):
            tiles = token_tiles(l, "out")
            w = 0 if stage == "mix" else 1
            for s in sides(l):
                for h in range(2):
                    wait_copied(dve, ("GB", l, w, s, h))
            for n, t in enumerate(tiles):
                dve.wait_ge(sem(f"post_{stage}{l}"), 2 * n + 2)
                link(dve.reciprocal(rstd[:, t:t + 1], std[:, t:t + 1]))
                dve.scalar_tensor_tensor(y(t), y(t), rstd[:, t:t + 1], gate[:, w, 0 if t < 2 else 1, :], ALU.mult,
                                         ALU.mult).then_inc(sem(f"y_{stage}{l}"), 1)
                if t % 2:
                    dve.wait_ge(sem(f"y_{stage}{l}"), n + 1)
                    dve.tensor_tensor(X[:, t, :], X[:, t, :], y(t), ALU.add).then_inc(x_added(stage, l, t), 1)

        def dense_ffn():
            for j in range(UP_UNITS):
                split_upto(U["up", 0] + j + 2)
                wait_copied(dve, ("GU", 0, j, 0))
                key = ("GU", 0, j, 1)
                wait_filled(dve, key)
                empties(dve.tensor_tensor(ffnT[:, j, :], ffn_sil[:, j % 2, :], bank(key), ALU.mult), key)
            for f in range(FT):
                split_upto(U["down", 0] + (f + 1) // 2 + 1)
                dve.wait_ge(sem("ffn_hi"), f + 1)
                dve.tensor_tensor(ffn_lo[:, f % 2, :], ffnT[:, f, :], ffn_hi[:, f % 2, :].bitcast(F32),
                                  ALU.subtract).then_inc(sem("ffn_lo"), 1)

        for l in range(DEPTH):
            if l == 0:
                for n, here in enumerate(mod_steps([(0, j) for j in range(MOD_A)])):
                    for key in here:
                        mod_step(*key)
                    if 2 <= n < 2 + TILES:
                        norm(0, "mix", (n - 2,))
                lambdas()
            else:
                norm(l, "mix")
            low_parts(l, "mix", 0)
            in_projection(l)
            attention(l)
            split_upto(U["mod_b", l] + MOD_UNITS - MOD_A + 1)
            gla(l)
            split_upto(U["out", l] + 1)
            low_parts(l, "out", token_tiles(l, "out")[0] * P)
            split_upto(U["out", l] + OUT_UNITS + 1)
            residual(l, "mix", y_mix_of)
            norm(l, "ffn")
            if l == 0:
                low_parts(l, "ffn", 0)
                dense_ffn()
                residual(l, "ffn", y_ffn_of)

        for q in range(4):
            key = ("H2", q)
            part = slice((q % 2) * 512, (q % 2 + 1) * 512)
            dve.wait_ge(sem("h2_hi"), q + 1)
            empties(dve.tensor_tensor(h2_lo[:, q // 2, part], bank(key), h2_hi[:, q // 2, part].bitcast(F32),
                                      ALU.subtract), key)
        link(dve.memset(y_moe[:, :, :], 0.0))
        link(dve.memset(route[:, :, :, :], 0.0))
        link(dve.memset(counts_i[:, :], 0))
        field = lambda i: route[:, :, i, 0:EXPERTS]
        two = lambda i: rt[:, 2 * i:2 * i + 2]
        wide = lambda a: a.unsqueeze(2).to_broadcast([P, 2, EXPERTS])
        LOGIT, FIRST, SECOND, TAKEN, POSITION, WEIGHT = range(6)
        descending = const[:, C_DESC:C_DESC + EXPERTS].unsqueeze(1).to_broadcast([P, 2, EXPERTS])
        key = ("LG",)
        wait_filled(dve, key)
        empties(dve.tensor_copy(field(LOGIT), bank(key)[:, 0:2 * EXPERTS].rearrange("p (t e) -> p t e", t=2)), key)
        wait_copied(dve, key)
        for n, pick in enumerate((FIRST, SECOND)):
            link(dve.tensor_reduce(two(n), field(LOGIT), X_AXIS, ALU.max))
            link(dve.tensor_tensor(field(pick), field(LOGIT), wide(two(n)), ALU.is_equal))
            link(dve.tensor_tensor(field(pick), field(pick), descending, ALU.mult))
            link(dve.tensor_reduce(two(3), field(pick), X_AXIS, ALU.max))
            link(dve.tensor_tensor(field(pick), field(pick), wide(two(3)), ALU.is_equal))
            if n == 0:
                link(dve.scalar_tensor_tensor(field(LOGIT), field(FIRST), -3.0e38, field(LOGIT), ALU.mult, ALU.add))
        dve.tensor_tensor(two(2), two(1), two(0), ALU.subtract).then_inc(sem("top_gap"), 1)
        dve.tensor_tensor(field(TAKEN), field(FIRST), field(SECOND), ALU.add).then_inc(sem("taken"), 1)
        dve.wait_ge(sem("top_exp"), 1)
        link(dve.tensor_scalar(two(4), two(2), 1.0, None, ALU.add))
        link(dve.reciprocal(two(4), two(4)))
        link(dve.tensor_tensor(two(5), two(4), two(2), ALU.mult))
        link(dve.tensor_tensor(field(FIRST), field(FIRST), wide(two(4)), ALU.mult))
        link(dve.tensor_tensor(field(SECOND), field(SECOND), wide(two(5)), ALU.mult))
        link(dve.tensor_tensor(field(WEIGHT), field(FIRST), field(SECOND), ALU.add))
        key = ("POS",)
        wait_filled(dve, key)
        dve.tensor_copy(field(POSITION), bank(key)[:, 0:2 * EXPERTS].rearrange("p (t e) -> p t e", t=2))
        empties(dve.tensor_copy(counts_i[:, 0:EXPERTS], bank(key)[:, 2 * EXPERTS:3 * EXPERTS]), key)
        wait_copied(dve, key)
        for tau in range(2):
            dve.sem_inc(esem("added", tau), 1)

        def select(e):
            dve.tensor_copy(e_cols[:, :].rearrange("p (t f) -> p t f", t=2),
                            route[:, :, 3:5, bass.ds(e, 1)].rearrange("p t f a -> p t (f a)")).then_inc(sem("e_cols"), 1)
            dve.wait_ge(sem("e_cols"), e + 1)
            for tt in range(2):
                dve.tensor_scalar(sel[:, tt, :], const[:, C_IOTA:C_IOTA + 2 * P], e_cols[:, 2 * tt + 1:2 * tt + 2],
                                  e_cols[:, 2 * tt:2 * tt + 1], ALU.is_equal, ALU.mult).then_inc(sem("sel"), 1)

        def split_expert(e, start, stop):
            for m in range(start, stop):
                n = U["moe", 1] + m
                for half, part in enumerate(HALVES):
                    dve.wait_ge(hi_ready, e * (2 * EXPERT_UNITS) + (2 * n + half + 1))
                    ins = dve.tensor_tensor(w_lo[:, n % RING, part], raw[:, n % RING, part],
                                            w_hi[:, n % RING, part].bitcast(F32), ALU.subtract)
                ins.then_inc(lo_ready, 1)

        def columns_low(e, tau):
            for b in range(2):
                dve.wait_ge(esem("xt_hi", tau), e * 2 + (b + 1))
                dve.tensor_tensor(xt_lo[:, 4 * b:4 * b + 4, tau, :], psum[:, b, :].rearrange("p (k n) -> p k n", n=P),
                                  xt_hi[:, 4 * b:4 * b + 4, tau, :].bitcast(F32), ALU.subtract).then_inc(esem("xt_lo", tau), 1)

        select(0)
        split_expert(0, 0, RING)
        many = dve.value_load(counts_i[0:1, 0:1], min_val=0, max_val=LAT) > P
        both(dve, many, lambda tau: columns_low(0, tau), [("xt_lo", 2)])
        with dve.Fori(0, EXPERTS) as e:
            many = dve.value_load(counts_i[0:1, bass.ds(e, 1)], min_val=0, max_val=LAT) > P
            many_next = dve.value_load(counts_i[0:1, bass.ds(e + 1, 1)], min_val=0, max_val=LAT) > P

            def product(c, tau):
                dve.wait_ge(esem("sil", tau), e * FC + (c + 1))
                if c >= 2:
                    dve.wait_ge(esem("turn", tau), e * FC + (c - 1))
                dve.tensor_tensor(e_act[:, tau, c % 2, :], e_sil[:, tau, :], psum[:, up_bank(c, tau), 256:512],
                                  ALU.mult).then_inc(esem("act", tau), 1)

            def turned(c, tau):
                dve.wait_ge(esem("eT_hi", tau), e * FC + (c + 1))
                dve.tensor_tensor(eT_lo[:, tau, c % 2, :], psum[:, TURN_BANK, 0:256],
                                  eT_hi[:, tau, c % 2, :].bitcast(F32), ALU.subtract).then_inc(esem("eT_lo", tau), 1)

            def output(tau):
                for h in range(2):
                    dve.wait_ge(esem("ey_hi", tau), e * 2 + (h + 1))
                    part = slice(h * 512, (h + 1) * 512)
                    dve.tensor_tensor(ey_lo[:, part], psum[:, 4 + 2 * tau + h, :], ey_hi[:, part].bitcast(F32),
                                      ALU.subtract).then_inc(esem("ey_lo", tau), 1)

            def added(tau):
                for n in range(4):
                    tt, part = n // 2, slice((n % 2) * 512, (n % 2 + 1) * 512)
                    dve.wait_ge(esem("scatter", tau), e * 4 + (n + 1))
                    if tau:
                        dve.wait_ge(esem("added", 0), e * 4 + (n + 2))
                    dve.scalar_tensor_tensor(y_moe[:, tt, part], psum[:, scatter_bank(n, tau), :],
                                             e_weight[:, tt:tt + 1], y_moe[:, tt, part], ALU.mult,
                                             ALU.add).then_inc(esem("added", tau), 1)

            for tau in range(2):
                dve.wait_ge(esem("added", tau), e * 4 + 1)
            dve.tensor_copy(e_weight[:, :].unsqueeze(2), route[:, :, 5, bass.ds(e, 1)]).then_inc(sem("e_weight"), 1)
            done = RING
            for c in range(FC):
                split_expert(e, done, STEPS[c]["up"][1] + RING)
                done = STEPS[c]["up"][1] + RING
                both(dve, many, lambda tau: product(c, tau), [("act", 1)])
                if c:
                    both(dve, many, lambda tau: turned(c - 1, tau), [("eT_lo", 1)])
                if c == FC // 2:
                    for tau in range(2):
                        dve.wait_ge(esem("selT", tau), e + 1)
                    dve.wait_ge(sem("sel"), e * 2 + 2)
                    select(e + 1)
            split_expert(e, done, EXPERT_UNITS + 1)
            both(dve, many, lambda tau: turned(FC - 1, tau), [("eT_lo", 1)])
            split_expert(e, EXPERT_UNITS + 1, EXPERT_UNITS + 2)
            dve.wait_ge(sem("e_weight"), e + 1)

            output(0)
            both(dve, many_next, lambda tau: columns_low(e + 1, tau), [("xt_lo", 2)])
            added(0)
            with dve.If(many):
                output(1)
                added(1)
                dve.nop()
            with dve.Else():
                dve.sem_inc(esem("ey_lo", 1), 2)
                dve.sem_inc(esem("added", 1), 4)
            split_expert(e, EXPERT_UNITS + 2, EXPERT_UNITS + 3)
        for tau in range(2):
            dve.wait_ge(esem("added", tau), EXPERTS * 4 + 1)
        residual(1, "ffn", y_moe_of)

    @block.tensor
    def _(pe):
        def three(dst, lhs, rhs, first, last):
            for n, (a, b) in enumerate(PASSES):
                ins = pe.matmul(dst, lhs(a), rhs(b), start=first and n == 0, stop=last and n == 2)
            return ins

        def unit(n):
            pe.wait_ge(lo_ready, n + 1)
            return n % RING

        def mod_step(kind, l, j):
            key = (kind, l, j)
            if kind == "mod":
                s = unit(mod_unit(l, j))
                wait_emptied(pe, key)
                for k in range(KT):
                    for part_of in range(2):
                        ins = pe.matmul(bank(key)[0:4, 0:256], c_cols[:, k, :], weights[part_of][:, s, k * 256:(k + 1) * 256],
                                        start=k == 0 and part_of == 0, stop=k == KT - 1 and part_of == 1)
            else:
                wait_copied(pe, ("mod", l, j))
                wait_emptied(pe, key)
                for i in range(2):
                    ins = pe.matmul(bank(key)[:, 2 * i:2 * i + 2], mod_row[:, i * P:(i + 1) * P],
                                    const[0:4, C_SELC:C_SELC + 2], start=True, stop=True)
            ins.then_inc(filled, 1)

        def beside_item(l, stage, place):
            for key in beside(l, stage).get(place, ()):
                mod_step(*key)

        def gates_on_all(l, w):
            pe.wait_ge(sem(f"gate_cols{l}"), 4 * (w + 1))
            for s in sides(l):
                for h in range(2):
                    key = ("GB", l, w, s, h)
                    wait_emptied(pe, key)
                    for k in range(4):
                        column = modc[:, l, 3 * w + 2, 4 * h + k, s:s + 1].to_broadcast([P, P])
                        ins = pe.matmul(bank(key)[:, k * P:(k + 1) * P], column, ident, start=True, stop=True)
                    ins.then_inc(filled, 1)

        def turn(l, stage):
            tiles = token_tiles(l, stage)
            pe.wait_ge(sem(f"xn_{stage}{l}"), len(tiles))
            for k in range(KT):
                key = ("T", l, stage, k)
                wait_emptied(pe, key)
                for t in tiles:
                    ins = pe.transpose(bank(key)[:, t * P:(t + 1) * P], xn[:, t, k * P:(k + 1) * P], ident)
                ins.then_inc(filled, 1)

        def gate_logits(l):
            wait_copied(pe, ("glr", l))
            pe.wait_ge(gw2_loaded, 16 * (l + 1))
            pe.wait_ge(sem("zeros"), 2)
            for t in range(TILES):
                key = ("Z", l, t)
                wait_emptied(pe, key)
                pe.matmul(bank(key), glrT[0:33, t * P:(t + 1) * P], gw2[0:33, :], start=True, stop=True).then_inc(filled, 1)

        def gate_sums(l):
            pe.wait_ge(sem(f"gl{l}"), TILES)
            for dp in range(4):
                key, d = ("G", l, dp), dp // 2
                wait_emptied(pe, key)
                for t in range(TILES):
                    ins = pe.matmul(bank(key)[:, t * P:(t + 1) * P], gl[:, t, dp * P:(dp + 1) * P],
                                    const[:, C_TRI + d * P:C_TRI + (d + 1) * P], start=True, stop=True)
                ins.then_inc(filled, 1)

        def in_projection(l):
            for u in range(IN_F):
                s = unit(U["in", l] + u)
                for i in range(2):
                    key = ("F", l, 2 * u + i)
                    wait_emptied(pe, key)
                    for k in range(KT):
                        pe.wait_ge(sem(f"act_lo_mix{l}"), k + 1)
                        ins = three(bank(key), lambda a: weights[a][:, s, k * 256 + i * P:k * 256 + (i + 1) * P],
                                    lambda b: acts[b][:, k, :], k == 0, k == KT - 1)
                    ins.then_inc(filled, 1)
            rotate(l)
            key = ("glr", l)
            pe.wait_ge(sem(f"glr_lo{l}"), 1)
            wait_emptied(pe, key)
            for k in range(KT):
                ins = three(bank(key)[0:32, :], lambda a: (glr_hi, glr_lo)[a][:, k, :], lambda b: acts[b][:, k, :],
                            k == 0, k == KT - 1)
            ins.then_inc(filled, 1)
            for u in range(IN_K):
                s = unit(U["in", l] + IN_F + u)
                for g in range(2):
                    key = ("K", l, u, g)
                    wait_emptied(pe, key)
                    for i in range(2):
                        for k in range(KT):
                            ins = three(bank(key)[:, i * 256:(i + 1) * 256],
                                        lambda a: acts[a][:, k, (2 * g + i) * P:(2 * g + i + 1) * P],
                                        lambda b: weights[b][:, s, k * 256:(k + 1) * 256], k == 0, k == KT - 1)
                    ins.then_inc(filled, 1)
                if u == Z_AFTER:
                    gate_logits(l)
                if u == G_AFTER:
                    gate_sums(l)

        def rotate(l):
            for b in range(4):
                key = ("rope", l, b)
                src = qT if b < 2 else kT
                wait_emptied(pe, key)
                for i in range(2):
                    h = 2 * (b % 2) + i
                    wait_copied(pe, ("F", l, h + (0 if b < 2 else 4)))
                    ins = pe.matmul(bank(key)[:, i * 256:(i + 1) * 256], const[:, C_PERM:C_PERM + P], src[:, h, CTX:T],
                                    start=True, stop=True)
                ins.then_inc(filled, 1)

        def attention(l):
            items = attn_items(l)
            n = len(items)
            pe.wait_ge(sem(f"roped{l}"), 4)
            for g in range(2):
                for u in range(2):
                    wait_copied(pe, ("K", l, u, g))
            for i in range(n + 2):
                if i < n:
                    h, t = items[i]
                    keys = n_keys(t)
                    for j in range(2):
                        key = ("S", l, i, j)
                        wait_emptied(pe, key)
                        r = slice(j * QK, (j + 1) * QK)
                        pe.matmul(bank(key)[:, 0:keys], qT[r, h, t * P:(t + 1) * P], kT[r, h, 0:keys], start=True,
                                  stop=True).then_inc(filled, 1)
                beside_item(l, "att", 2 * i)
                if 1 <= i <= n:
                    key, keys = ("PT", l, i - 1), n_keys(items[i - 1][1])
                    pe.wait_ge(sem(f"probs{l}"), i)
                    wait_emptied(pe, key)
                    for k in range(keys // P):
                        ins = pe.transpose(bank(key)[:, k * P:(k + 1) * P], probs[:, (i - 1) % 2, 0, k * P:(k + 1) * P], ident)
                    ins.then_inc(filled, 1)
                if i >= 2:
                    key, (h, t) = ("O", l, i - 2), items[i - 2]
                    wait_copied(pe, ("PT", l, i - 2))
                    wait_emptied(pe, key)
                    tiles = n_keys(t) // P
                    for k in range(tiles):
                        ins = pe.matmul(bank(key)[:, 0:P], probsT[:, i % 2, k * P:(k + 1) * P], v[:, k, h * P:(h + 1) * P],
                                        start=k == 0, stop=k == tiles - 1)
                    ins.then_inc(filled, 1)
                beside_item(l, "att", 2 * i + 1)

        def gla(l):
            for u in range(2, 4):
                for g in range(2):
                    wait_copied(pe, ("K", l, u, g))
            for dp in range(4):
                pair = dp % 2
                key = ("KT", l, dp)
                pe.wait_ge(sem(f"gmul{l}"), 4 * dp + 1)
                wait_emptied(pe, key)
                for t in range(TILES):
                    ins = pe.transpose(bank(key)[:, t * P:(t + 1) * P], gexp[:, 2, dp, t * P:(t + 1) * P], ident)
                ins.then_inc(filled, 1)
            for dp in range(4):
                pair = dp % 2
                wait_copied(pe, ("KT", l, dp))
                for half in range(2):
                    key = ("DS", l, dp, half)
                    wait_emptied(pe, key)
                    r = slice(half * CHUNK, (half + 1) * CHUNK)
                    for t in range(TILES):
                        for hh in range(2):
                            ins = pe.matmul(bank(key)[hh * QK:(hh + 1) * QK, t * P:(t + 1) * P],
                                            klT[r, dp, t, hh * QK:(hh + 1) * QK],
                                            gv[r, t, (2 * pair + hh) * P:(2 * pair + hh + 1) * P], start=True, stop=True)
                    ins.then_inc(filled, 1)
            pe.wait_ge(sem(f"gmul{l}"), 16)
            items = gla_items(l)
            for i in range(len(items) + 1):
                if i < len(items):
                    h, t = items[i]
                    pair, r = h // 2, slice((h % 2) * QK, (h % 2 + 1) * QK)
                    key = ("M", l, i)
                    wait_emptied(pe, key)
                    for d in range(2):
                        dp = 2 * d + pair
                        ins = pe.matmul(bank(key)[:, d * P:(d + 1) * P], gexp[r, 1, dp, t * P:(t + 1) * P],
                                        gexp[r, 0, dp, t * P:(t + 1) * P], start=True, stop=True)
                    ins.then_inc(filled, 1)
                beside_item(l, "gla", 2 * i)
                if i >= 1:
                    h, t = items[i - 1]
                    pair, r = h // 2, slice((h % 2) * QK, (h % 2 + 1) * QK)
                    key = ("OG", l, i - 1)
                    wait_copied(pe, ("M", l, i - 1))
                    if i == 1:
                        for dp in range(4):
                            for half in range(2):
                                wait_copied(pe, ("DS", l, dp, half))
                    wait_emptied(pe, key)
                    for d in range(2):
                        pe.matmul(bank(key)[:, 0:P], Am[:, (i - 1) % 2, d, :], gv[:, t, h * P:(h + 1) * P],
                                  start=d == 0, stop=False, skip_group_check=True)
                    parts = [(half, d) for half in range(2) for d in range(2)
                             if 2 * t + half != chunk_order(d)[0]]
                    for n, (half, d) in enumerate(parts):
                        c = 2 * t + half
                        ins = pe.matmul(bank(key)[half * CHUNK:(half + 1) * CHUNK, 0:P],
                                        gexp[r, 3, 2 * d + pair, c * CHUNK:(c + 1) * CHUNK], states[r, 2 * d + pair, c, :],
                                        start=False, stop=n == len(parts) - 1, skip_group_check=True)
                    ins.then_inc(filled, 1)

        def out_projection(l):
            tiles = token_tiles(l, "out")
            pe.wait_ge(sem(f"merged{l}"), 2)
            for f in range(KT):
                key = ("MT", l, f)
                src = od if f < 4 else og
                wait_emptied(pe, key)
                for t in tiles:
                    ins = pe.transpose(bank(key)[:, t * P:(t + 1) * P], src[:, t, (f % 4) * P:(f % 4 + 1) * P], ident)
                ins.then_inc(filled, 1)
            for u in range(OUT_UNITS):
                s = unit(U["out", l] + u)
                for g in range(2 if l == 0 else 1):
                    key = ("Y", l, u, g)
                    wait_emptied(pe, key)
                    for i in range(2):
                        t = (2 * g if l == 0 else 2) + i
                        for k in range(KT):
                            pe.wait_ge(sem(f"act_lo_out{l}"), k + 1)
                            ins = three(bank(key)[:, i * 256:(i + 1) * 256], lambda a: acts[a][:, k, t * P:(t + 1) * P],
                                        lambda b: weights[b][:, s, k * 256:(k + 1) * 256], k == 0, k == KT - 1)
                    ins.then_inc(filled, 1)

        def dense_ffn():
            for j in range(UP_UNITS):
                s = unit(U["up", 0] + j)
                for i in range(2):
                    key = ("GU", 0, j, i)
                    wait_emptied(pe, key)
                    for k in range(KT):
                        if j == 0 and i == 0:
                            pe.wait_ge(sem("act_lo_ffn0"), k + 1)
                        ins = three(bank(key), lambda a: weights[a][:, s, k * 256 + i * P:k * 256 + (i + 1) * P],
                                    lambda b: acts[b][:, k, :], k == 0, k == KT - 1)
                    ins.then_inc(filled, 1)
            for t in range(TILES):
                for h in range(2):
                    wait_emptied(pe, ("D", 0, t, h))
            for f in range(FT):
                s = unit(U["down", 0] + f // 2)
                pe.wait_ge(sem("ffn_lo"), f + 1)
                for t in range(TILES):
                    for h in range(2):
                        c0 = (f % 2) * D_MODEL + h * 512
                        ins = three(bank(("D", 0, t, h)), lambda a: (ffn_hi, ffn_lo)[a][:, f % 2, t * P:(t + 1) * P],
                                    lambda b: weights[b][:, s, c0:c0 + 512], f == 0, f == FT - 1)
                        if f == FT - 1:
                            ins.then_inc(filled, 1)
                if f < FT - 1:
                    ins.then_inc(sem("down_tiles"), 1)

        pe.wait_ge(sem("c_lo"), 2)
        for l in range(DEPTH):
            if l == 0:
                for n, here in enumerate(mod_steps([(0, j) for j in range(MOD_A)])):
                    if n == 1:
                        pe.wait_ge(const_loaded, 16)
                    for key in here:
                        mod_step(*key)
            turn(l, "mix")
            in_projection(l)
            attention(l)
            gla(l)
            gates_on_all(l, 0)
            out_projection(l)
            gates_on_all(l, 1)
            turn(l, "ffn")
            if l == 0:
                dense_ffn()

        for q in range(4):
            key, tt = ("H2", q), q // 2
            wait_emptied(pe, key)
            for k in range(4):
                kk = 4 * (q % 2) + k
                wait_copied(pe, ("T", 1, "ffn", kk))
                ins = pe.transpose(bank(key)[:, k * P:(k + 1) * P], h2T[:, kk, tt * P:(tt + 1) * P], ident)
            ins.then_inc(filled, 1)
        key = ("LG",)
        wait_emptied(pe, key)
        for tt in range(2):
            for k in range(KT):
                ins = pe.matmul(bank(key)[:, tt * EXPERTS:(tt + 1) * EXPERTS], h2T[:, k, tt * P:(tt + 1) * P],
                                wsm[:, 512 + k * EXPERTS:512 + (k + 1) * EXPERTS], start=k == 0, stop=k == KT - 1)
        ins.then_inc(filled, 1)
        key = ("POS",)
        pe.wait_ge(sem("taken"), 1)
        wait_emptied(pe, key)
        upper = const[:, C_UPPER:C_UPPER + P]
        for field_at, parts in ((0, ((upper, 0),)), (1, ((ones, 0), (upper, 1))), (2, ((ones, 0), (ones, 1)))):
            for n, (lhs, tt) in enumerate(parts):
                ins = pe.matmul(bank(key)[:, field_at * EXPERTS:(field_at + 1) * EXPERTS], lhs, route[:, tt, 3, 0:EXPERTS],
                                start=n == 0, stop=n == len(parts) - 1)
        ins.then_inc(filled, 1)
        wait_copied(pe, ("POS",))
        for tau in range(2):
            for name in ("half", "up", "down"):
                pe.sem_inc(esem(name, tau), FC)
            pe.sem_inc(esem("act", tau), 1)

        def gather_rows(e, tau):
            if tau == 0:
                pe.wait_ge(sem("sel"), e * 2 + 2)
                pe.wait_ge(esem("act", 0), e * FC + 1)
            else:
                pe.wait_ge(esem("xt_hi", 0), e * 2 + 2)
                pe.wait_ge(esem("xt_lo", 0), e * 2 + 2)
            for b in range(2):
                for n in range(4):
                    src, tt = (h2_hi, h2_lo)[n // 2], n % 2
                    ins = pe.matmul(psum[:, b, :], sel[:, tt, tau * P:(tau + 1) * P], src[:, tt, b * 512:(b + 1) * 512],
                                    start=n == 0, stop=n == 3)
                ins.then_inc(esem("rows", tau), 1)

        def gather_columns(e, tau):
            pe.wait_ge(esem("rows_copy", tau), e * 2 + 2)
            for b in range(2):
                for k in range(4):
                    ins = pe.transpose(psum[:, b, k * P:(k + 1) * P], e_rows[:, (4 * b + k) * P:(4 * b + k + 1) * P], ident)
                ins.then_inc(esem("columns", tau), 1)

        def gather_second(e, many):
            with pe.If(many):
                gather_rows(e, 1)
                gather_columns(e, 1)
                pe.nop()
            with pe.Else():
                pe.sem_inc(esem("rows", 1), 2)
                pe.sem_inc(esem("columns", 1), 2)

        many = pe.value_load(counts_i[0:1, 0:1], min_val=0, max_val=LAT) > P
        gather_rows(0, 0)
        gather_columns(0, 0)
        gather_second(0, many)
        with pe.Fori(0, EXPERTS) as e:
            many = pe.value_load(counts_i[0:1, bass.ds(e, 1)], min_val=0, max_val=LAT) > P
            many_next = pe.value_load(counts_i[0:1, bass.ds(e + 1, 1)], min_val=0, max_val=LAT) > P

            def eunit(m):
                n = U["moe", 1] + m
                pe.wait_ge(lo_ready, e * EXPERT_UNITS + (n + 1))
                return n % RING

            def up(c, half, s, tau):
                if half == 0:
                    if c == 0:
                        for i in range(2):
                            pe.wait_ge(esem("xt_lo", i), e * 2 + 2)
                        if tau:
                            for i in range(2):
                                pe.wait_ge(esem("added", i), e * 4 + 1)
                    elif tau == 0 and c >= 2:
                        pe.wait_ge(esem("act", 0), e * FC + c)
                    elif tau:
                        pe.wait_ge(esem("act", 1), e * FC + (c + 1))
                for kk in range(4):
                    k = 4 * half + kk
                    ins = three(psum[:, up_bank(c, tau), :], lambda a: (xt_hi, xt_lo)[a][:, k, tau, :],
                                lambda b: weights[b][:, s, kk * 512:(kk + 1) * 512], k == 0, k == KT - 1)
                ins.then_inc(esem(("half", "up")[half], tau), 1)

            def turn_sel(tau):
                for i in range(2):
                    pe.wait_ge(esem("added", i), e * 4 + 1)
                if tau:
                    pe.wait_ge(esem("selT_copy", 0), e + 1)
                for tt in range(2):
                    ins = pe.transpose(psum[:, TURN_BANK, tt * P:(tt + 1) * P],
                                       sel[:, tt, tau * P:(tau + 1) * P].bitcast(F32), ident)
                ins.then_inc(esem("selT", tau), 1)

            def turned(c, tau):
                pe.wait_ge(esem("act", tau), e * FC + (c + 2))
                if tau:
                    pe.wait_ge(esem("eT_lo", 0), e * FC + (c + 1))
                elif c:
                    for i in range(2):
                        pe.wait_ge(esem("eT_lo", i), e * FC + c)
                else:
                    for i in range(2):
                        pe.wait_ge(esem("selT_copy", i), e + 1)
                for j in range(2):
                    ins = pe.transpose(psum[:, TURN_BANK, j * P:(j + 1) * P], e_act[:, tau, c % 2, j * P:(j + 1) * P], ident)
                ins.then_inc(esem("turn", tau), 1)

            def down(c, s, tau):
                pe.wait_ge(esem("eT_lo", tau), e * FC + (c + 1))
                for j in range(2):
                    for h in range(2):
                        ins = three(psum[:, 4 + 2 * tau + h, :],
                                    lambda a: (eT_hi, eT_lo)[a][:, tau, c % 2, j * P:(j + 1) * P],
                                    lambda b: weights[b][:, s, j * D_MODEL + h * 512:j * D_MODEL + (h + 1) * 512],
                                    c == 0 and j == 0, c == FC - 1 and j == 1)
                ins.then_inc(esem("down", tau), 1)

            def scatter(tau):
                pe.wait_ge(esem("selT_copy", tau), e + 1)
                if tau == 0:
                    pe.wait_ge(esem("act", 1), (e + 1) * FC + 1)
                    for i in range(2):
                        pe.wait_ge(esem("eT_lo", i), (e + 1) * FC)
                for n in range(4):
                    tt, h = divmod(n, 2)
                    pe.wait_ge(esem("ey_lo", tau), e * 2 + (h + 1))
                    if tau and n < 2:
                        pe.wait_ge(esem("added", 0), e * 4 + (n + 2))
                    for i, src in enumerate((ey_hi, ey_lo)):
                        ins = pe.matmul(psum[:, scatter_bank(n, tau), :], selT[:, tau, tt, :], src[:, h * 512:(h + 1) * 512],
                                        start=i == 0, stop=i == 1)
                    ins.then_inc(esem("scatter", tau), 1)

            for c in range(FC + 2):
                here = STEPS[c]
                if c < FC:
                    for half in range(2):
                        s = eunit(here["up"][half])
                        both(pe, many, lambda tau: up(c, half, s, tau), [(("half", "up")[half], 1)])
                    if c == 0:
                        both(pe, many, turn_sel, [("selT", 1)])
                    elif c == 1:
                        both(pe, many, lambda tau: turned(0, tau), [("turn", 1)])
                if "down" in here:
                    s = eunit(here["down"])

                    def turned_and_down(tau):
                        if c < FC:
                            turned(c - 1, tau)
                        down(c - 2, s, tau)

                    both(pe, many, turned_and_down, [("turn", 1), ("down", 1)] if c < FC else [("down", 1)])
                if c == FC:
                    both(pe, many, lambda tau: turned(c - 1, tau), [("turn", 1)])
                if c == FC:
                    gather_rows(e + 1, 0)
            gather_columns(e + 1, 0)
            gather_second(e + 1, many_next)
            both(pe, many, scatter, [("scatter", 4)])


def constants():
    import numpy as np
    c = np.zeros((P, N_CONST), np.float32)
    i = np.arange(P)
    c[:, C_IDENT:C_IDENT + P] = np.eye(P)
    same = (i[:, None] // CHUNK) == (i[None, :] // CHUNK)
    c[:, C_TRI:C_TRI + P] = (same & (i[:, None] <= i[None, :])) / 16.0
    c[:, C_TRI + P:C_TRI + 2 * P] = (same & (i[:, None] >= i[None, :])) / 16.0
    c[:, C_UPPER:C_UPPER + P] = i[:, None] < i[None, :]
    c[:, C_ONES:C_ONES + P] = 1.0
    partner = np.where(i % 32 < 16, i + 16, i - 16)
    c[partner, C_PERM + i] = 1.0
    c[:, C_IOTA:C_IOTA + 2 * P] = np.arange(2 * P)
    c[2:4, C_SELC] = 1.0
    c[0:2, C_SELC + 1] = 1.0
    c[:, C_EPS] = EPS
    c[:, C_DESC:C_DESC + EXPERTS] = np.arange(EXPERTS, 0, -1)
    return c


def rope_constants():
    import numpy as np
    n_freq = QK // 4
    inv = (np.float32(ROPE_THETA) ** (-np.arange(n_freq, dtype=np.float32) / np.float32(n_freq))).astype(np.float32)
    token, feature = np.arange(LAT), np.arange(P)
    place = np.where((feature[:, None] % QK) < QK // 2, token // GRID_W, token % GRID_W).astype(np.float32)
    angle = place * inv[feature % n_freq][:, None]
    sign = np.where(feature % 32 < 16, -1.0, 1.0).astype(np.float32)[:, None]
    return np.ascontiguousarray(np.stack([np.cos(angle), np.sin(angle) * sign], 1).astype(np.float32))


def pack(inputs):
    import numpy as np
    a = {k: np.asarray(x) for k, x in inputs.items()}

    def by_rows(w):
        return w.reshape(KT, P, 256).transpose(1, 0, 2).reshape(P, UNIT)

    units = np.empty((N_UNITS, P, UNIT), np.float32)
    n = 0

    def put(w):
        nonlocal n
        units[n] = w
        n += 1

    in_columns = [0, 256, 512, 768, 1536, 1792, 1024, 1280, 2048, 2304, 2560, 2816]
    for stage, l in STAGES:
        if stage in ("mod_a", "mod_b"):
            for j in range(MOD_A) if stage == "mod_a" else range(MOD_A, MOD_UNITS):
                put(by_rows(a["w_mod"][l][:, j * 256:(j + 1) * 256]))
        elif stage == "in":
            for c in in_columns:
                put(by_rows(a["w_in"][l][:, c:c + 256]))
        elif stage == "out":
            for u in range(OUT_UNITS):
                put(by_rows(a["w_out"][l][:, u * 256:(u + 1) * 256]))
        elif stage == "up":
            for j in range(UP_UNITS):
                put(by_rows(np.concatenate([a[w][0][:, j * P:(j + 1) * P] for w in ("ffn_w1", "ffn_w3")], 1)))
        elif stage == "down":
            for i in range(DOWN_UNITS):
                put(a["ffn_w2"][0][i * 256:(i + 1) * 256].reshape(2, P, D_MODEL).transpose(1, 0, 2).reshape(P, UNIT))
        else:
            for e in range(EXPERTS):
                for c in range(FC + 2):
                    if c < FC:
                        both = np.concatenate([a[w][0, e][:, c * 256:(c + 1) * 256] for w in ("moe_w1", "moe_w3")], 1)
                        both = both.reshape(2, 4, P, 512)
                        for half in range(2):
                            put(both[half].transpose(1, 0, 2).reshape(P, UNIT))
                    if c >= 2:
                        put(a["moe_w2"][0, e][(c - 2) * 256:(c - 1) * 256].reshape(2, P, D_MODEL)
                            .transpose(1, 0, 2).reshape(P, UNIT))
    assert n == N_UNITS

    cols = np.zeros((P, N_COLS), np.float32)
    col = lambda x: x.reshape(-1, P).T
    cols[:, V_C:V_C + 8], cols[:, V_CC:V_CC + 8] = col(a["c"][0]), col(a["c_ctx"])
    wsm = np.zeros((P, 576), np.float32)
    gw2 = np.zeros((DEPTH, 33, T), np.float32)
    for l in range(DEPTH):
        b = V_LAYER + l * V_STRIDE
        cols[:, b + V_GPM:b + V_GPM + 8], cols[:, b + V_GPF:b + V_GPF + 8] = col(a["g_pre_mix"][l]), col(a["g_pre_ffn"][l])
        cols[:, b + V_SUB], cols[:, b + V_ON] = a["diff_subln"][l], a["gla_onorm"][l]
        cols[:, b + V_BMOD:b + V_BMOD + 48] = col(a["b_mod"][l])
        wsm[:, l * 256:(l + 1) * 256] = a["w_in"][l][:, 3072:].reshape(KT, P, 32).transpose(1, 0, 2).reshape(P, 256)
        for d in range(2):
            gw2[l, d * RANK:(d + 1) * RANK, d * 256:(d + 1) * 256] = a["gla_gate_w2"][l, d]
        gw2[l, 32] = a["gla_gate_b"][l].reshape(-1)
        for i, g in enumerate(("g_post_mix", "g_post_ffn")):
            cols[:, b + V_POST + 8 * i:b + V_POST + 8 * (i + 1)] = col(a[g][l])
    wsm[:, 512:] = a["router"][0].reshape(KT, P, EXPERTS).transpose(1, 0, 2).reshape(P, 64)
    return {
        "units": units, "x_in": np.ascontiguousarray(a["x"][0]), "ctx_in": np.ascontiguousarray(a["ctx"][0]),
        "const_in": constants(), "cols_in": cols, "wsm_in": wsm, "gw2_in": gw2,
        "lam_in": np.ascontiguousarray(a["diff_lambda"].reshape(1, -1)), "rope_in": rope_constants(),
    }


def kernel(**inputs):
    import concourse.bacc as bacc
    from concourse.bass_utils import run_bass_kernel_spmd as run

    arrays = pack(inputs)
    nc = bacc.Bacc("TRN2", target_bir_lowering=False, num_devices=1)
    args = {k: nc.dram_tensor(k, x.shape, F32, kind="ExternalInput").ap() for k, x in arrays.items()}
    out = nc.dram_tensor("out", (1, LAT, D_MODEL), F32, kind="ExternalOutput").ap()
    with ExitStack() as ctx:
        build(nc, ctx, *(args[k] for k in ("units", "x_in", "ctx_in", "const_in", "cols_in", "wsm_in", "gw2_in",
                                           "lam_in", "rope_in")), out)
    return run(nc, [arrays], core_ids=[0]).results[0]["out"]
```
